# Optimizing a Trainium2 kernel written in Bass

```python
import math
import jax, jax.numpy as jnp
from jax import lax
import numpy as np

D_MODEL = 2048
BATCH = 1
SEQ = 512
DEPTH = 1

MIX_WIDTH = D_MODEL
ATTN_WIDTH = D_MODEL // 2
CONV_WIDTH = MIX_WIDTH - ATTN_WIDTH
DIFF_HEAD_DIM = 64
N_DIFF_HEADS = ATTN_WIDTH // (2 * DIFF_HEAD_DIM)
DIFF_V_DIM = 2 * DIFF_HEAD_DIM
Q_BLOCK = 128
CONV_K = 3
IN_COLS = 3 * ATTN_WIDTH + 3 * CONV_WIDTH
PEER_HEADS = 8
PEER_N_KEYS = 128
PEER_N_EXPERTS = PEER_N_KEYS * PEER_N_KEYS
PEER_QUERY_DIM = 256
PEER_HALF = PEER_QUERY_DIM // 2
PEER_TOPK = 16
TOKEN_BLOCK = 128
EPS = 1e-6

kernel_name = "hymba_diffattn_shortconv_peer"

def _rms(x, g):
    xf = x.astype(jnp.float32)
    y = xf * lax.rsqrt(jnp.mean(xf * xf, axis=-1, keepdims=True) + EPS)
    return (y * g.astype(jnp.float32)).astype(x.dtype)

def _alibi_slopes(n):
    return jnp.exp2(-8.0 * jnp.arange(1, n + 1, dtype=jnp.float32) / n)

def _diff_attention(q, k, v, lam):
    b, s, h, _, d = q.shape
    nb = s // Q_BLOCK
    scale = 1.0 / math.sqrt(d)
    slopes = _alibi_slopes(h)
    key_pos = jnp.arange(s, dtype=jnp.int32)
    q_blocks = jnp.moveaxis(q.reshape(b, nb, Q_BLOCK, h, 2, d), 1, 0)
    starts = jnp.arange(nb, dtype=jnp.int32) * Q_BLOCK

    def one_block(args):
        qb, start = args
        scores = jnp.einsum("bqhcd,bkhcd->bhcqk", qb, k).astype(jnp.float32) * scale
        q_pos = start + jnp.arange(Q_BLOCK, dtype=jnp.int32)
        dist = (q_pos[:, None] - key_pos[None, :]).astype(jnp.float32)
        scores = scores - slopes[:, None, None, None] * dist
        scores = jnp.where(dist >= 0, scores, -jnp.inf)
        p = jax.nn.softmax(scores, axis=-1)
        a = p[:, :, 0] - lam * p[:, :, 1]
        return jnp.einsum("bhqk,bkhe->bqhe", a.astype(v.dtype), v)

    out = lax.map(one_block, (q_blocks, starts))
    return jnp.moveaxis(out, 0, 1).reshape(b, s, h, v.shape[-1])

def _short_conv(bg, cg, xc, w):
    s = xc.shape[1]
    u = cg * xc
    up = jnp.pad(u, ((0, 0), (CONV_K - 1, 0), (0, 0)))
    y = up[:, 0:s] * w[0]
    for j in range(1, CONV_K):
        y = y + up[:, j:j + s] * w[j]
    return bg * y

def _peer(h, w_q, subkeys, u, v):
    b, s, dm = h.shape
    t = b * s
    ht = h.reshape(t, dm)
    q = (ht @ w_q).reshape(t, PEER_HEADS, 2, PEER_HALF)
    sc = jnp.einsum("thcd,hckd->thck", q, subkeys).astype(jnp.float32)
    s1, i1 = lax.top_k(sc[:, :, 0], PEER_TOPK)
    s2, i2 = lax.top_k(sc[:, :, 1], PEER_TOPK)
    cand = (s1[..., :, None] + s2[..., None, :]).reshape(t, PEER_HEADS, PEER_TOPK * PEER_TOPK)
    top, idx = lax.top_k(cand, PEER_TOPK)
    e1 = jnp.take_along_axis(i1, idx // PEER_TOPK, axis=-1)
    e2 = jnp.take_along_axis(i2, idx % PEER_TOPK, axis=-1)
    experts = (e1 * PEER_N_KEYS + e2).reshape(t, PEER_HEADS * PEER_TOPK)
    gates = jax.nn.softmax(top, axis=-1).reshape(t, PEER_HEADS * PEER_TOPK)
    nblk = t // TOKEN_BLOCK

    def one_block(args):
        hb, eb, gb = args
        ug = jnp.take(u, eb, axis=0)
        vg = jnp.take(v, eb, axis=0)
        act = jax.nn.gelu(jnp.einsum("tkd,td->tk", ug, hb), approximate=False) * gb.astype(hb.dtype)
        return jnp.einsum("tk,tkd->td", act, vg)

    out = lax.map(one_block, (ht.reshape(nblk, TOKEN_BLOCK, dm),
                              experts.reshape(nblk, TOKEN_BLOCK, -1),
                              gates.reshape(nblk, TOKEN_BLOCK, -1)))
    return out.reshape(b, s, dm)

def setup_inputs(seed: int = 0) -> dict:
    key = jax.random.key(seed)
    ks = jax.random.split(key, 17)

    def nrm(k, shape, scale):
        return jax.random.normal(k, shape, jnp.float32) * scale

    return {
        "x": nrm(ks[0], (BATCH, SEQ, D_MODEL), 1.0),
        "attn_norm_g": 1.0 + nrm(ks[1], (DEPTH, D_MODEL), 0.02),
        "w_in": nrm(ks[2], (DEPTH, D_MODEL, IN_COLS), D_MODEL ** -0.5),
        "q_norm_g": 1.0 + nrm(ks[3], (DEPTH, DIFF_HEAD_DIM), 0.02),
        "k_norm_g": 1.0 + nrm(ks[4], (DEPTH, DIFF_HEAD_DIM), 0.02),
        "lambda_q1": nrm(ks[5], (DEPTH, DIFF_HEAD_DIM), 0.1),
        "lambda_k1": nrm(ks[6], (DEPTH, DIFF_HEAD_DIM), 0.1),
        "lambda_q2": nrm(ks[7], (DEPTH, DIFF_HEAD_DIM), 0.1),
        "lambda_k2": nrm(ks[8], (DEPTH, DIFF_HEAD_DIM), 0.1),
        "subln_g": 1.0 + nrm(ks[9], (DEPTH, DIFF_V_DIM), 0.02),
        "conv_w": nrm(ks[10], (DEPTH, CONV_K, CONV_WIDTH), CONV_K ** -0.5),
        "w_out": nrm(ks[11], (DEPTH, MIX_WIDTH, D_MODEL), MIX_WIDTH ** -0.5),
        "ffn_norm_g": 1.0 + nrm(ks[12], (DEPTH, D_MODEL), 0.02),
        "peer_w_q": nrm(ks[13], (DEPTH, D_MODEL, PEER_HEADS * PEER_QUERY_DIM), D_MODEL ** -0.5),
        "peer_subkeys": nrm(ks[14], (DEPTH, PEER_HEADS, 2, PEER_N_KEYS, PEER_HALF), PEER_HALF ** -0.5),
        "peer_u": nrm(ks[15], (DEPTH, PEER_N_EXPERTS, D_MODEL), D_MODEL ** -0.5),
        "peer_v": nrm(ks[16], (DEPTH, PEER_N_EXPERTS, D_MODEL), 0.5),
    }

def reference(x, attn_norm_g, w_in, q_norm_g, k_norm_g, lambda_q1, lambda_k1, lambda_q2, lambda_k2,
              subln_g, conv_w, w_out, ffn_norm_g, peer_w_q, peer_subkeys, peer_u, peer_v):
    b, s, _ = x.shape
    splits = [ATTN_WIDTH, 2 * ATTN_WIDTH, 3 * ATTN_WIDTH,
              3 * ATTN_WIDTH + CONV_WIDTH, 3 * ATTN_WIDTH + 2 * CONV_WIDTH]
    for l in range(DEPTH):
        h = _rms(x, attn_norm_g[l])
        proj = h @ w_in[l]
        q, k, v, cb, cc, cx = jnp.split(proj, splits, axis=-1)
        q = _rms(q.reshape(b, s, N_DIFF_HEADS, 2, DIFF_HEAD_DIM), q_norm_g[l])
        k = _rms(k.reshape(b, s, N_DIFF_HEADS, 2, DIFF_HEAD_DIM), k_norm_g[l])
        v = v.reshape(b, s, N_DIFF_HEADS, DIFF_V_DIM)
        lam_init = 0.8 - 0.6 * math.exp(-0.3 * l)
        lam = (jnp.exp(jnp.sum(lambda_q1[l].astype(jnp.float32) * lambda_k1[l].astype(jnp.float32)))
               - jnp.exp(jnp.sum(lambda_q2[l].astype(jnp.float32) * lambda_k2[l].astype(jnp.float32)))
               + lam_init)
        a = _diff_attention(q, k, v, lam)
        a = (_rms(a, subln_g[l]) * (1.0 - lam_init)).reshape(b, s, ATTN_WIDTH)
        c = _short_conv(cb, cc, cx, conv_w[l])
        x = x + jnp.concatenate([a, c], axis=-1) @ w_out[l]
        x = x + _peer(_rms(x, ffn_norm_g[l]), peer_w_q[l], peer_subkeys[l], peer_u[l], peer_v[l])
    return x


_drawn_inputs = setup_inputs


def setup_inputs(seed=0):
    import zlib

    import numpy as np

    out = dict(_drawn_inputs(seed))
    spreads = {}
    factors = {'k_norm_g': 3.005, 'lambda_q1': 156.227, 'subln_g': 2.811, 'ffn_norm_g': 2.93}
    for name, (base, spread) in spreads.items():
        noise = np.random.default_rng([zlib.crc32(name.encode()), seed]).standard_normal(out[name].shape)
        drawn = base * np.exp(spread * noise) if base else spread * noise
        out[name] = __import__('jax').numpy.asarray(drawn.astype(out[name].dtype))
    for name, factor in factors.items():
        out[name] = (out[name] * factor).astype(out[name].dtype)
    return out
```

```python
from contextlib import ExitStack
import math

import concourse.bass as bass
from concourse import mybir

F32 = mybir.dt.float32
U32 = mybir.dt.uint32
ALU = mybir.AluOpType
ACT = mybir.ActivationFunctionType
AX = mybir.AxisListType

P = 128
SEQ = 512
D = 2048
KT = D // P
TB = SEQ // P
ATTN = D // 2
CONV = D - ATTN
HEADS = 8
HD = 64
VD = 2 * HD
CT = CONV // P
TAPS = 3
CHUNK = 512
PEER_HEADS = 8
N_KEYS = 128
N_EXPERTS = N_KEYS * N_KEYS
HALF = 128
TOPK = 16
RING = 4
EPS = 1e-6
LAM_INIT = 0.8 - 0.6 * math.exp(-0.3 * 0)
MASKED = -1.0e30
LOWEST = -3.0e38

V_Q, V_K, V_SUB, V_CONV = 0, 1, 2, 3
N_VEC = V_CONV + TAPS * CT

assert CT == HEADS and VD == P and HALF == P and N_KEYS == P


class Steps:

    def __init__(self, engine, sem):
        self.engine, self.sem, self.base, self.n = engine, sem, 0, 0

    def done(self, instruction):
        instruction.then_inc(self.sem, 1)
        self.n += 1
        return self.base + self.n

    def link(self, instruction):
        self.engine.wait_ge(self.sem, self.done(instruction))

    def enter(self, i, per):
        self.outside, self.first, self.per = self.base, self.n, per
        self.base = self.base + i * per

    def leave(self, trips):
        assert self.n - self.first == self.per, f"{self.n - self.first} steps, not {self.per}"
        self.base = self.outside + (trips - 1) * self.per


def decoder_layer(nc, x, attn_norm_g, w_in, q_norm_g, k_norm_g, lambda_q1, lambda_k1, lambda_q2, lambda_k2,
                  subln_g, conv_w, w_out, ffn_norm_g, peer_w_q, peer_subkeys, peer_u, peer_v, out):
    ctx = ExitStack()
    with ctx:
        def sb(name, shape, dt=F32):
            return ctx.enter_context(nc.sbuf_tensor(name, shape, dt))

        def sem(name):
            return ctx.enter_context(nc.semaphore(name))

        def sems(name, n):
            return [sem(f"{name}{i}") for i in range(n)]

        x_v = x[0].rearrange("(t p) d -> t p d", p=P)
        out_v = out[0].rearrange("(t p) d -> t p d", p=P)
        w_in_v = w_in[0].rearrange("(k p) n -> p k n", p=P)
        w_out_v = w_out[0].rearrange("(k p) n -> p k n", p=P)
        w_q_v = peer_w_q[0].rearrange("(k p) n -> p k n", p=P)
        subkeys_v = peer_subkeys[0].rearrange("h c k d -> k (h c) d")
        u_table, v_table = peer_u[0], peer_v[0]

        region_a = sb("region_a", [P, KT * SEQ])
        hT = region_a[:, :].rearrange("p (k t) -> p k t", k=KT)
        region_b = sb("region_b", [P, KT * CHUNK])
        w_half = [region_b[:, i * 4096:(i + 1) * 4096].rearrange("p (k n) -> p k n", n=CHUNK) for i in range(2)]
        w_conv = [region_b[:, i * 2048:(i + 1) * 2048].rearrange("p (k n) -> p k n", n=P) for i in range(3)]
        u_rows = [region_b[:, i * D:(i + 1) * D] for i in range(RING)]
        region_c = sb("region_c", [P, TB * 3 * ATTN])
        qkv = region_c[:, :].rearrange("p (t n) -> p t n", t=TB)
        x_rows = region_c[:, 0:TB * D].rearrange("p (t d) -> p t d", t=TB)
        w_peer = region_c[:, TB * D:TB * D + KT * 2 * HALF].rearrange("p (k n) -> p k n", k=KT)
        region_d = sb("region_d", [P, TB * D])
        h_rows = region_d[:, :].rearrange("p (t d) -> p t d", t=TB)
        mixT = region_d[:, :].rearrange("p (k t) -> p k t", k=KT)
        region_f = sb("region_f", [P, RING * D])
        v_rows = [region_f[:, i * D:(i + 1) * D] for i in range(RING)]
        squares = region_f[:, 0:D]
        qk_n = region_f[:, 0:1024].rearrange("p (a n) -> p a n", a=2)
        sq = region_f[:, 1024:2048].rearrange("p (a n) -> p a n", a=2)
        conv_u, conv_y = region_f[:, 1024:1536], region_f[:, 1536:2048]
        qkT = region_f[:, 2048:3072].rearrange("p (a n) -> p a n", a=2)
        probs = region_f[:, 3072:5120].rearrange("p (s c n) -> p s c n", s=2, c=2)
        aT = region_f[:, 5120:6144].rearrange("p (s n) -> p s n", s=2)
        o_sq, o_n = region_f[:, 6144:6656], region_f[:, 6656:7168]
        b_sb, c_sb = region_f[:, 7168:7680], region_f[:, 7680:8192]
        region_g = sb("region_g", [P, D])
        gain = region_g[:, :]
        diag = region_g[:, :].rearrange("p (s n) -> p s n", s=TOPK)

        ident = sb("ident", [P, P])
        iota16 = sb("iota16", [P, TOPK])
        alibi = sb("alibi", [P, SEQ])
        vec_rows = sb("vec_rows", [N_VEC, P])
        vec = sb("vec", [P, N_VEC])
        lam_in = sb("lam_in", [P, 4, HD])
        lam_prod = sb("lam_prod", [P, HD])
        lam = sb("lam", [P, 4])
        neg_lam = sb("neg_lam", [P, 1])
        ssq = sb("ssq", [P, 2 * TB])
        rstd = sb("rstd", [P, 2 * TB])
        qk_ss = sb("qk_ss", [P, 16])
        minus_half = sb("minus_half", [P, 16])
        conv_taps = sb("conv_taps", [P, TAPS, 1])
        row_max = sb("row_max", [P, 2, 2])
        neg_max = sb("neg_max", [P, 2, 2])
        row_sum = sb("row_sum", [P, 2, 2])
        inv_sum = sb("inv_sum", [P, 2, 2])
        o_ss = sb("o_ss", [P, TB])
        pqT = sb("pqT", [P, 2, SEQ])
        keys = sb("keys", [P, 2, HALF])
        keysT = sb("keysT", [P, 2, N_KEYS])
        key_scores = sb("key_scores", [P, 2, TB, N_KEYS])
        rest = sb("rest", [P, N_KEYS])
        half_top = sb("half_top", [P, 2, TOPK])
        half_idx = sb("half_idx", [P, 2, TOPK], U32)
        half_num = sb("half_num", [P, 2, TOPK])
        cand = sb("cand", [P, TOPK, TOPK])
        cand_rest = sb("cand_rest", [P, TOPK * TOPK])
        top = sb("top", [P, TOPK])
        top_idx = sb("top_idx", [P, TOPK], U32)
        pair = sb("pair", [P, 2, TOPK], U32)
        pair_num = sb("pair_num", [P, 2, TOPK])
        pick = sb("pick", [P, 2, TOPK, TOPK])
        picked = sb("picked", [P, 2, TOPK])
        neg_top = sb("neg_top", [P, 1])
        experts = sb("experts", [P, TB, TOPK], U32)
        gates = sb("gates", [P, TB, TOPK])
        gate_sum = sb("gate_sum", [P, 1])
        gate_inv = sb("gate_inv", [P, 1])
        dots = sb("dots", [P, TOPK])
        gelus = sb("gelus", [P, TOPK])
        acts = sb("acts", [P, TOPK])

        ps = ctx.enter_context(nc.psum_tensor("ps", [P, 8, CHUNK], F32))
        ps_rows = ps[:, 0:TB, :].rearrange("p b n -> p (b n)")
        ps_pq = ps[:, 4:6, :]
        ps_keysT = ps[:, 4, 0:2 * P].rearrange("p (c n) -> p c n", c=2)
        ps_key_scores = ps[:, 6:8, :].rearrange("p c (t n) -> p c t n", t=TB)

        const_step = sem("const_step")
        x_in = sems("x_in", TB)
        gain_in = sem("gain_in")
        vec_in = sem("vec_in")
        vec_ps = sem("vec_ps")
        vec_ready = sem("vec_ready")
        lam_sum = sem("lam_sum")
        lam_exp = sem("lam_exp")
        ssq_ready = sem("ssq_ready")
        mean_ready = sem("mean_ready")
        rstd_ready = sem("rstd_ready")
        qk_mean = sem("qk_mean")
        qk_rstd = sem("qk_rstd")
        o_mean = sem("o_mean")
        o_rstd = sem("o_rstd")
        h_ready = sem("h_ready")
        hT_ps = sem("hT_ps")
        hT_by_act = sem("hT_by_act")
        hT_by_dve = sem("hT_by_dve")
        w_in_half = sems("w_in_half", 2)
        w_half0_used = sem("w_half0_used")
        proj_done = sems("proj_done", TB)
        proj_kept = sems("proj_kept", TB)
        cw_in = sems("cw_in", 3)
        conv_done = sems("conv_done", 3)
        b_kept = sem("b_kept")
        c_kept = sem("c_kept")
        conv_gated = sem("conv_gated")
        conv_out = sem("conv_out")
        qk_normed = sem("qk_normed")
        qkT_ps = sem("qkT_ps")
        qkT_ready = sem("qkT_ready")
        scores_done = sem("scores_done")
        scores_read = sems("scores_read", 2)
        max_ready = sem("max_ready")
        exp_done = sem("exp_done")
        a_ready = sem("a_ready")
        a_turned = sems("a_turned", 2)
        aT_ready = sem("aT_ready")
        av_done = sems("av_done", 2)
        o_squared = sem("o_squared")
        o_normed = sem("o_normed")
        oT_ps = sem("oT_ps")
        o_out = sem("o_out")
        wo_half = sems("wo_half", 2)
        wo_half0_used = sem("wo_half0_used")
        out_done = sems("out_done", TB)
        out_added = sems("out_added", TB)
        wq_in = sem("wq_in")
        wq_used = sem("wq_used")
        keys_in = sem("keys_in")
        keys_used = sem("keys_used")
        pqT_ready = sem("pqT_ready")
        keysT_ready = sem("keysT_ready")
        key_scores_ps = sem("key_scores_ps")
        key_scores_ready = sem("key_scores_ready")
        key_scores_read = sem("key_scores_read")
        experts_ready = sem("experts_ready")
        top_ready = sem("top_ready")
        gates_exp = sem("gates_exp")
        u_in = sems("u_in", RING)
        u_used = sems("u_used", RING)
        v_in = sems("v_in", RING)
        v_used = sems("v_used", RING)
        gelu_done = sem("gelu_done")
        diag_ready = sem("diag_ready")
        rows_added = sem("rows_added")
        out_stored = sem("out_stored")
        dve_step = sem("dve_step")
        act_step = sem("act_step")
        pool_past = sem("pool_past")
        dve_past = sem("dve_past")
        nc_block = ctx.enter_context(nc.Block())

        @nc_block.sync
        def _(sp):
            for t in range(TB):
                sp.dma_start(x_rows[:, t, :], x_v[t]).then_inc(x_in[t], 16)
                if t == 0:
                    sp.dma_start(gain, attn_norm_g[0:1, :].to_broadcast([P, D])).then_inc(gain_in, 16)
            with sp.Fori(0, 3 * ATTN // CHUNK) as c:
                for i in range(2):
                    sp.wait_ge(w_half0_used if i == 0 else proj_done[TB - 1], c)
                    sp.dma_start(w_half[i], w_in_v[:, 8 * i:8 * i + 8, bass.ds(c * CHUNK, CHUNK)])\
                        .then_inc(w_in_half[i], 16)
            sp.wait_ge(w_half0_used, 3 * ATTN // CHUNK)
            sp.wait_ge(proj_done[TB - 1], 3 * ATTN // CHUNK)
            with sp.Fori(0, CT) as j:
                for s in range(3):
                    sp.wait_ge(conv_done[s], j)
                    sp.dma_start(w_conv[s], w_in_v[:, :, bass.ds(j * P + (3 * ATTN + s * CONV), P)])\
                        .then_inc(cw_in[s], 16)
            sp.wait_ge(h_ready, TB)
            sp.dma_start(gain, ffn_norm_g[0:1, :].to_broadcast([P, D])).then_inc(gain_in, 16)
            sp.wait_ge(av_done[1], 2 * HEADS)
            sp.wait_ge(qk_normed, 2 * HEADS)
            for t in range(TB):
                sp.dma_start(x_rows[:, t, :], x_v[t]).then_inc(x_in[t], 16)
            for s in range(3):
                sp.wait_ge(conv_done[s], CT)
            with sp.Fori(0, D // CHUNK) as c:
                for i in range(2):
                    sp.wait_ge(wo_half0_used if i == 0 else out_done[TB - 1], c)
                    sp.dma_start(w_half[i], w_out_v[:, 8 * i:8 * i + 8, bass.ds(c * CHUNK, CHUNK)])\
                        .then_inc(wo_half[i], 16)
            with sp.Fori(0, PEER_HEADS) as h:
                sp.wait_ge(wq_used, h)
                sp.dma_start(w_peer, w_q_v[:, :, bass.ds(h * 2 * HALF, 2 * HALF)]).then_inc(wq_in, 16)
                sp.wait_ge(keys_used, h)
                sp.dma_start(keys[:, :, :], subkeys_v[:, bass.ds(h * 2, 2), :]).then_inc(keys_in, 16)
            for t in range(TB):
                sp.wait_ge(rows_added, (PEER_HEADS - 1) * TB + t + 1)
                sp.dma_start(out_v[t], x_rows[:, t, :]).then_inc(out_stored, 16)
            sp.wait_ge(out_stored, 16 * TB)

        @nc_block.gpsimd
        def _(pool):
            pool.memset(ident[:, :], 0.0).then_inc(const_step, 1)
            pool.iota(iota16[:, :], [[1, TOPK]], base=0, channel_multiplier=0,
                      allow_small_or_imprecise_dtypes=True).then_inc(const_step, 1)
            pool.iota(alibi[:, :], [[1, SEQ]], base=-(SEQ - P), channel_multiplier=-1,
                      allow_small_or_imprecise_dtypes=True).then_inc(const_step, 1)
            pool.memset(minus_half[:, :], -0.5).then_inc(const_step, 1)
            pool.wait_ge(const_step, 4)
            pool.affine_select(out=ident[:, :], in_=ident[:, :], compare_op=ALU.not_equal, fill=1.0,
                               base=0, pattern=[[-1, P]], channel_multiplier=1).then_inc(const_step, 1)
            pool.affine_select(out=alibi[:, :], in_=alibi[:, :], compare_op=ALU.is_ge, fill=MASKED,
                               base=SEQ - P, pattern=[[-1, SEQ]], channel_multiplier=1).then_inc(const_step, 1)
            for i, row in ((0, q_norm_g), (1, k_norm_g)):
                for c in range(2):
                    pool.dma_start(vec_rows[i:i + 1, c * HD:(c + 1) * HD], row[0:1, :]).then_inc(vec_in, 16)
            pool.dma_start(vec_rows[V_SUB:V_SUB + 1, :], subln_g[0:1, :]).then_inc(vec_in, 16)
            pool.dma_start(vec_rows[V_CONV:N_VEC, :], conv_w[0].rearrange("j (c p) -> (j c) p", p=P))\
                .then_inc(vec_in, 16)
            for i, row in enumerate((lambda_q1, lambda_k1, lambda_q2, lambda_k2)):
                pool.dma_start(lam_in[:, i, :], row[0:1, :].to_broadcast([P, HD])).then_inc(vec_in, 16)

            def inverse_root(a):
                return nc.gpsimd.tensor_tensor(a, a, minus_half[:, 0:a.shape[1]], ALU.pow)

            def norm(n):
                for i in range(n * TB, (n + 1) * TB):
                    pool.wait_ge(mean_ready, i + 1)
                    inverse_root(rstd[:, i:i + 1]).then_inc(rstd_ready, 1)

            norm(0)
            with pool.Fori(0, HEADS) as j:
                pool.wait_ge(qk_mean, j + 1)
                inverse_root(qk_ss[:, :]).then_inc(qk_rstd, 1)
                pool.wait_ge(o_mean, j + 1)
                inverse_root(o_ss[:, :]).then_inc(o_rstd, 1)
            norm(1)

            def gather_u(unit, t, s):
                pool.wait_ge(u_used[s % RING], 4 * unit + s // RING)
                pool.sem_inc(pool_past, 1)
                pool.indirect_dma_start(
                    out=u_rows[s % RING], out_offset=None, in_=u_table,
                    in_offset=bass.IndirectOffsetOnAxis(ap=experts[:, t, s:s + 1], axis=0))\
                    .then_inc(u_in[s % RING], 16)

            def gather_v(unit, t, s):
                pool.wait_ge(v_used[s % RING], 4 * unit + s // RING)
                pool.sem_inc(pool_past, 1)
                pool.indirect_dma_start(
                    out=v_rows[s % RING], out_offset=None, in_=v_table,
                    in_offset=bass.IndirectOffsetOnAxis(ap=experts[:, t, s:s + 1], axis=0))\
                    .then_inc(v_in[s % RING], 16)

            def head(h, last):
                for t in range(TB):
                    unit = TB * h + t
                    ahead = not (last and t == TB - 1)
                    if ahead:
                        pool.wait_ge(experts_ready, unit + 2)
                        pool.sem_inc(pool_past, 1)
                    for s in range(TOPK):
                        if ahead:
                            gather_u(unit + 1, (t + 1) % TB, s)
                        gather_v(unit, t, s)

            pool.wait_ge(experts_ready, 1)
            pool.sem_inc(pool_past, 1)
            for s in range(TOPK):
                gather_u(0, 0, s)
            with pool.Fori(0, PEER_HEADS - 1) as h:
                head(h, last=False)
            head(PEER_HEADS - 1, last=True)

        @nc_block.scalar
        def _(act):
            steps = Steps(act, act_step)

            def norm(n):
                for t in range(TB + 1):
                    if t < TB:
                        if n == 0:
                            act.wait_ge(x_in[t], 16)
                        else:
                            act.wait_ge(out_added[t], D // CHUNK)
                        if n * TB + t > 0:
                            act.wait_ge(ssq_ready, n * TB + t)
                        nc.scalar.activation(squares, x_rows[:, t, :], ACT.Square,
                                             accum_out=ssq[:, n * TB + t:n * TB + t + 1]).then_inc(ssq_ready, 1)
                    if t > 0:
                        act.wait_ge(hT_ps, n * TB + t)
                        for b in range(2):
                            nc.scalar.activation(hT[:, 4 * b:4 * b + 4, (t - 1) * P:t * P],
                                                 ps[:, 4 + b, :].rearrange("p (k t) -> p k t", k=4),
                                                 ACT.Copy).then_inc(hT_by_act, 1)

            act.wait_ge(lam_sum, 1)
            nc.scalar.activation(lam[:, 2:4], lam[:, 0:2], ACT.Exp).then_inc(lam_exp, 1)
            norm(0)
            with act.Fori(0, 3 * ATTN // CHUNK) as c:
                for t in (0, 2):
                    act.wait_ge(proj_done[t], c + 1)
                    nc.scalar.activation(qkv[:, t, bass.ds(c * CHUNK, CHUNK)], ps[:, t, :], ACT.Copy)\
                        .then_inc(proj_kept[t], 1)
            act.wait_ge(vec_ready, 1)
            with act.Fori(0, HEADS) as j:
                def exps(qb):
                    act.wait_ge(max_ready, TB * j + qb + 1)
                    for c in range(2):
                        part = probs[:, qb % 2, c, 0:(qb + 1) * P]
                        nc.scalar.activation(part, part, ACT.Exp, bias=neg_max[:, qb % 2, c:c + 1],
                                             accum_out=row_sum[:, qb % 2, c:c + 1]).then_inc(exp_done, 1)

                def keep_aT(qb):
                    act.wait_ge(a_turned[qb % 2], 2 * j + qb // 2 + 1)
                    act.wait_ge(av_done[qb % 2], 2 * j + qb // 2)
                    nc.scalar.activation(aT[:, qb % 2, 0:(qb + 1) * P], ps[:, 6, 0:(qb + 1) * P], ACT.Copy)\
                        .then_inc(aT_ready, 1)

                act.wait_ge(conv_done[0], j + 1)
                act.wait_ge(conv_out, j)
                nc.scalar.activation(b_sb, ps[:, 0, :], ACT.Copy).then_inc(b_kept, 1)
                for i in range(2):
                    act.wait_ge(qkT_ps, 2 * j + i + 1)
                    nc.scalar.activation(qkT[:, i, :], ps[:, 6 + i, :], ACT.Copy,
                                         scale=vec[:, V_Q + i:V_Q + i + 1]).then_inc(qkT_ready, 1)
                exps(0)
                exps(1)
                keep_aT(0)
                exps(2)
                act.wait_ge(conv_done[1], j + 1)
                act.wait_ge(conv_gated, j)
                nc.scalar.activation(c_sb, ps[:, 1, :], ACT.Copy).then_inc(c_kept, 1)
                keep_aT(1)
                exps(3)
                keep_aT(2)
                keep_aT(3)
                act.wait_ge(av_done[1], 2 * j + 2)
                nc.scalar.activation(o_sq, ps[:, 7, :], ACT.Square).then_inc(o_squared, 1)
                act.wait_ge(oT_ps, j + 1)
                nc.scalar.activation(mixT[:, bass.ds(j, 1), :], ps[:, 6:7, :], ACT.Copy,
                                     scale=vec[:, V_SUB:V_SUB + 1]).then_inc(o_out, 1)
            norm(1)

            def key_scoring(h):
                act.wait_ge(wq_used, h + 1)
                nc.scalar.activation(pqT[:, :, :], ps_pq, ACT.Copy).then_inc(pqT_ready, 1)
                act.wait_ge(keys_used, h + 1)
                nc.scalar.activation(keysT[:, :, :], ps_keysT, ACT.Copy).then_inc(keysT_ready, 1)
                act.wait_ge(key_scores_ps, h + 1)
                act.wait_ge(key_scores_read, TB * h)
                nc.scalar.activation(key_scores[:, :, :, :], ps_key_scores, ACT.Copy)\
                    .then_inc(key_scores_ready, 1)

            def gate_exp(unit, t):
                act.wait_ge(top_ready, unit + 1)
                nc.scalar.activation(gates[:, t, :], top[:, :], ACT.Exp, bias=neg_top[:, 0:1],
                                     accum_out=gate_sum[:, 0:1]).then_inc(gates_exp, 1)

            def gelu(unit):
                act.wait_ge(u_used[RING - 1], 4 * unit + 4)
                nc.scalar.activation(gelus[:, :], dots[:, :], ACT.Gelu).then_inc(gelu_done, 1)

            def head(h, last):
                for t in range(TB):
                    unit = TB * h + t
                    if t == 1 and not last:
                        key_scoring(h + 1)
                    if t == 0 or not last:
                        gate_exp(unit + 3, (t + 3) % TB)
                    if not (last and t == TB - 1):
                        gelu(unit + 1)

            key_scoring(0)
            for t in range(TB - 1):
                gate_exp(t, t)
            gelu(0)
            with act.Fori(0, PEER_HEADS - 1) as h:
                head(h, last=False)
            head(PEER_HEADS - 1, last=True)

        @nc_block.vector
        def _(dve):
            v = nc.vector
            steps = Steps(dve, dve_step)
            link, done = steps.link, steps.done

            def past():
                dve.sem_inc(dve_past, 1)

            def norm(n):
                for t in range(TB + 1):
                    i = n * TB + t
                    if t < TB:
                        dve.wait_ge(ssq_ready, i + 1)
                        v.tensor_scalar(rstd[:, i:i + 1], ssq[:, i:i + 1], 1.0 / D, EPS, ALU.mult, ALU.add)\
                            .then_inc(mean_ready, 1)
                        dve.wait_ge(rstd_ready, i + 1)
                        if t == 0:
                            dve.wait_ge(gain_in, 16 * (n + 1))
                        v.scalar_tensor_tensor(out=h_rows[:, t, :], in0=x_rows[:, t, :], scalar=rstd[:, i:i + 1],
                                               in1=gain, op0=ALU.mult, op1=ALU.mult).then_inc(h_ready, 1)
                    if t > 0:
                        dve.wait_ge(hT_ps, i)
                        for b in range(2, 4):
                            v.tensor_copy(hT[:, 4 * b:4 * b + 4, (t - 1) * P:t * P],
                                          ps[:, 4 + b, :].rearrange("p (k t) -> p k t", k=4)).then_inc(hT_by_dve, 1)

            dve.wait_ge(vec_in, 16 * 10)
            for i in range(2):
                link(v.tensor_tensor(lam_prod[:, :], lam_in[:, 2 * i, :], lam_in[:, 2 * i + 1, :], ALU.mult))
                ins = v.reduce_sum(lam[:, i:i + 1], lam_prod[:, :], axis=AX.X)
                if i == 0:
                    link(ins)
                else:
                    ins.then_inc(lam_sum, 1)
            dve.wait_ge(vec_ps, 1)
            link(v.tensor_copy(vec[:, :], ps[:, 3, 0:N_VEC]))
            link(v.tensor_scalar(vec[:, V_Q:V_Q + 1], vec[:, V_Q:V_Q + 1], HD ** -0.5, None, ALU.mult))
            v.tensor_scalar(vec[:, V_SUB:V_SUB + 1], vec[:, V_SUB:V_SUB + 1], 1.0 - LAM_INIT, None, ALU.mult)\
                .then_inc(vec_ready, 1)
            dve.wait_ge(lam_exp, 1)
            link(v.tensor_tensor(neg_lam[:, :], lam[:, 3:4], lam[:, 2:3], ALU.subtract))
            link(v.tensor_scalar(neg_lam[:, :], neg_lam[:, :], -LAM_INIT, None, ALU.add))
            norm(0)
            with dve.Fori(0, 3 * ATTN // CHUNK) as c:
                for t in (1, 3):
                    dve.wait_ge(proj_done[t], c + 1)
                    v.tensor_copy(qkv[:, t, bass.ds(c * CHUNK, CHUNK)], ps[:, t, :]).then_inc(proj_kept[t], 1)
            for t in range(TB):
                dve.wait_ge(proj_kept[t], 3 * ATTN // CHUNK)

            per_head = 21
            with dve.Fori(0, HEADS) as j:
                steps.enter(j, per_head)
                dve.wait_ge(qkT_ps, 2 * j)
                rows = [qkv[:, :, bass.ds(i * ATTN + j * P, P)] for i in range(2)]
                done(v.tensor_tensor(sq[:, 0, :].rearrange("p (t n) -> p t n", t=TB), rows[0], rows[0], ALU.mult))
                link(v.tensor_tensor(sq[:, 1, :].rearrange("p (t n) -> p t n", t=TB), rows[1], rows[1], ALU.mult))
                link(v.reduce_sum(qk_ss[:, :], sq.rearrange("p a (g d) -> p (a g) d", d=HD), axis=AX.X))
                v.tensor_scalar(qk_ss[:, :], qk_ss[:, :], 1.0 / HD, EPS, ALU.mult, ALU.add).then_inc(qk_mean, 1)
                dve.wait_ge(qk_rstd, j + 1)
                for i in range(2):
                    v.tensor_tensor(qk_n[:, i, :].rearrange("p (t c d) -> p t c d", t=TB, c=2),
                                    rows[i].rearrange("p t (c d) -> p t c d", c=2),
                                    qk_ss[:, 8 * i:8 * i + 8].rearrange("p (t c) -> p t c", c=2).unsqueeze(3)
                                    .to_broadcast([P, TB, 2, HD]), ALU.mult).then_inc(qk_normed, 1)
                done(v.tensor_scalar(alibi[:, :], alibi[:, :], 0.5, None, ALU.mult))
                link(v.tensor_copy(conv_taps[:, :, :],
                                   vec[:, V_CONV:N_VEC].rearrange("p (a c) -> p a c", a=TAPS)[:, :, bass.ds(j, 1)]))

                def biased(qb):
                    n = (qb + 1) * P
                    dve.wait_ge(scores_done, TB * j + qb + 1)
                    dve.wait_ge(a_turned[qb % 2], 2 * j + qb // 2)
                    past()
                    for c in range(2):
                        v.tensor_tensor_reduce(out=probs[:, qb % 2, c, 0:n], in0=ps[:, 2 + 2 * (qb % 2) + c, 0:n],
                                               in1=alibi[:, SEQ - n:SEQ], scale=1.0, scalar=LOWEST,
                                               op0=ALU.add, op1=ALU.max, accum_out=row_max[:, qb % 2, c:c + 1])\
                            .then_inc(scores_read[qb % 2], 1)
                    dve.wait_ge(scores_read[qb % 2], 4 * j + 2 * (qb // 2) + 2)
                    v.tensor_scalar(neg_max[:, qb % 2, :], row_max[:, qb % 2, :], -1.0, None, ALU.mult)\
                        .then_inc(max_ready, 1)

                def combined(qb):
                    n, i = (qb + 1) * P, qb % 2
                    dve.wait_ge(exp_done, 2 * (TB * j + qb) + 2)
                    link(v.reciprocal(inv_sum[:, i, :], row_sum[:, i, :]))
                    link(v.tensor_tensor(inv_sum[:, i, 1:2], inv_sum[:, i, 1:2], neg_lam[:, :], ALU.mult))
                    link(v.tensor_scalar(probs[:, i, 1, 0:n], probs[:, i, 1, 0:n], inv_sum[:, i, 1:2], None, ALU.mult))
                    past()
                    v.scalar_tensor_tensor(out=probs[:, i, 0, 0:n], in0=probs[:, i, 0, 0:n],
                                           scalar=inv_sum[:, i, 0:1], in1=probs[:, i, 1, 0:n],
                                           op0=ALU.mult, op1=ALU.add).then_inc(a_ready, 1)

                biased(0)
                biased(1)
                combined(0)
                biased(2)
                combined(1)
                biased(3)
                combined(2)
                combined(3)
                dve.wait_ge(o_squared, j + 1)
                link(v.reduce_sum(o_ss[:, :], o_sq.rearrange("p (t n) -> p t n", t=TB), axis=AX.X))
                v.tensor_scalar(o_ss[:, :], o_ss[:, :], 1.0 / VD, EPS, ALU.mult, ALU.add).then_inc(o_mean, 1)
                dve.wait_ge(o_rstd, j + 1)
                dve.wait_ge(oT_ps, j)
                v.tensor_tensor(o_n.rearrange("p (t n) -> p t n", t=TB),
                                ps[:, 7, :].rearrange("p (t n) -> p t n", t=TB),
                                o_ss[:, :].unsqueeze(2).to_broadcast([P, TB, VD]), ALU.mult).then_inc(o_normed, 1)
                dve.wait_ge(c_kept, j + 1)
                dve.wait_ge(conv_done[2], j + 1)
                v.tensor_tensor(conv_u, ps[:, 0, :], c_sb, ALU.mult).then_inc(conv_gated, 1)
                dve.wait_ge(conv_gated, j + 1)
                link(v.tensor_scalar(conv_y, conv_u, conv_taps[:, 2, :], None, ALU.mult))
                for lag in (1, 2):
                    past()
                    link(v.scalar_tensor_tensor(out=conv_y[:, lag:], in0=conv_u[:, 0:SEQ - lag],
                                                scalar=conv_taps[:, 2 - lag, :], in1=conv_y[:, lag:],
                                                op0=ALU.mult, op1=ALU.add))
                dve.wait_ge(b_kept, j + 1)
                v.tensor_tensor(mixT[:, bass.ds(j + HEADS, 1), :].squeeze(1), conv_y, b_sb, ALU.mult)\
                    .then_inc(conv_out, 1)
                dve.wait_ge(conv_out, j + 1)
                steps.leave(HEADS)
            for t in range(TB):
                dve.wait_ge(x_in[t], 32)
            with dve.Fori(0, D // CHUNK) as c:
                for t in range(TB):
                    part = x_rows[:, t, bass.ds(c * CHUNK, CHUNK)]
                    dve.wait_ge(out_done[t], c + 1)
                    v.tensor_tensor(part, ps[:, t, :], part, ALU.add).then_inc(out_added[t], 1)
            norm(1)

            def top16(values, indices, source, remains):
                past()
                link(v.max(values[:, 0:8], source))
                past()
                done(v.max_index(indices[:, 0:8], values[:, 0:8], source))
                link(v.match_replace(remains, values[:, 0:8], source, LOWEST))
                past()
                link(v.max(values[:, 8:16], remains))
                past()
                link(v.max_index(indices[:, 8:16], values[:, 8:16], remains))

            def choose_half(t, c):
                top16(half_top[:, c, :], half_idx[:, c, :], key_scores[:, c, t, :], rest[:, :])

            def choose_pairs(unit):
                v.tensor_scalar(half_num[:, 0, :], half_idx[:, 0, :], float(N_KEYS), None, ALU.mult)\
                    .then_inc(key_scores_read, 1)
                done(v.tensor_copy(half_num[:, 1, :], half_idx[:, 1, :]))
                link(v.tensor_tensor(cand[:, :, :],
                                     half_top[:, 0, :].unsqueeze(2).to_broadcast([P, TOPK, TOPK]),
                                     half_top[:, 1, :].unsqueeze(1).to_broadcast([P, TOPK, TOPK]), ALU.add))
                dve.wait_ge(gates_exp, unit)
                top16(top, top_idx, cand[:, :, :].rearrange("p a b -> p (a b)"), cand_rest[:, :])
                v.tensor_scalar(neg_top[:, :], top[:, 0:1], -1.0, None, ALU.mult).then_inc(top_ready, 1)

            def choose_experts(unit, t):
                done(v.tensor_scalar(pair[:, 0, :], top_idx[:, :], 4, None, ALU.logical_shift_right))
                link(v.tensor_scalar(pair[:, 1, :], top_idx[:, :], TOPK - 1, None, ALU.bitwise_and))
                link(v.tensor_copy(pair_num[:, :, :], pair[:, :, :]))
                link(v.tensor_tensor(pick[:, :, :, :].rearrange("p c s a -> p (c s) a"),
                                     pair_num[:, :, :].rearrange("p c s -> p (c s)").unsqueeze(2)
                                     .to_broadcast([P, 2 * TOPK, TOPK]),
                                     iota16[:, :].unsqueeze(1).to_broadcast([P, 2 * TOPK, TOPK]), ALU.is_equal))
                dve.wait_ge(key_scores_read, unit + 1)
                link(v.tensor_tensor(pick[:, :, :, :], pick[:, :, :, :],
                                     half_num[:, :, :].unsqueeze(2).to_broadcast([P, 2, TOPK, TOPK]), ALU.mult))
                link(v.reduce_sum(picked[:, :, :].rearrange("p c s -> p (c s)"),
                                  pick[:, :, :, :].rearrange("p c s a -> p (c s) a"), axis=AX.X))
                v.tensor_tensor(experts[:, t, :], picked[:, 0, :], picked[:, 1, :], ALU.add)\
                    .then_inc(experts_ready, 1)

            def finish_gates(unit, t):
                dve.wait_ge(gates_exp, unit + 1)
                link(v.reciprocal(gate_inv[:, :], gate_sum[:, :]))
                link(v.tensor_scalar(gates[:, t, :], gates[:, t, :], gate_inv[:, 0:1], None, ALU.mult))

            def dot(unit, t, s):
                dve.wait_ge(u_in[s % RING], 16 * (4 * unit + s // RING + 1))
                v.tensor_tensor_reduce(out=u_rows[s % RING], in0=u_rows[s % RING], in1=h_rows[:, t, :],
                                       scale=1.0, scalar=0.0, op0=ALU.mult, op1=ALU.add,
                                       accum_out=dots[:, s:s + 1]).then_inc(u_used[s % RING], 1)

            def weigh(unit, t):
                dve.wait_ge(gelu_done, unit + 1)
                link(v.tensor_tensor(acts[:, :], gelus[:, :], gates[:, t, :], ALU.mult))

            def spread():
                v.tensor_tensor(diag, ident[:, :].unsqueeze(1).to_broadcast([P, TOPK, P]),
                                acts[:, :].unsqueeze(2).to_broadcast([P, TOPK, P]), ALU.mult).then_inc(diag_ready, 1)

            def head(h, last):
                for t in range(TB):
                    unit = TB * h + t
                    ahead = not (last and t == TB - 1)
                    choosing = t == 0 or not last
                    chosen, ct = unit + 3, (t + 3) % TB
                    for s in range(TOPK):
                        if ahead:
                            dot(unit + 1, (t + 1) % TB, s)
                        if choosing and s == 4:
                            dve.wait_ge(key_scores_ready, h + (1 if t == 0 else 2))
                            past()
                            choose_half(ct, 0)
                        if choosing and s == 6:
                            choose_half(ct, 1)
                        if choosing and s == 8:
                            choose_pairs(chosen)
                        if choosing and s == 10:
                            choose_experts(chosen, ct)
                    if choosing:
                        finish_gates(chosen, ct)
                    if ahead:
                        weigh(unit + 1, (t + 1) % TB)
                    dve.wait_ge(v_used[RING - 1], 4 * unit + 4)
                    v.tensor_tensor(x_rows[:, t, :], ps_rows, x_rows[:, t, :], ALU.add).then_inc(rows_added, 1)
                    if ahead:
                        spread()

            dve.wait_ge(key_scores_ready, 1)
            for t in range(TB - 1):
                choose_half(t, 0)
                choose_half(t, 1)
                choose_pairs(t)
                choose_experts(t, t)
                finish_gates(t, t)
            for s in range(TOPK):
                dot(0, 0, s)
            weigh(0, 0)
            spread()
            per_head = 104
            with dve.Fori(0, PEER_HEADS - 1) as h:
                steps.enter(h, per_head)
                head(h, last=False)
                steps.leave(PEER_HEADS - 1)
            head(PEER_HEADS - 1, last=True)

        @nc_block.tensor
        def _(pe):
            mm, turn = nc.tensor.matmul, nc.tensor.transpose

            def norm(n):
                for t in range(TB):
                    pe.wait_ge(h_ready, n * TB + t + 1)
                    if n * TB + t > 0:
                        pe.wait_ge(hT_by_act, 2 * (n * TB + t))
                        pe.wait_ge(hT_by_dve, 2 * (n * TB + t))
                    for k in range(KT):
                        last = turn(ps[:, 4 + k // 4, (k % 4) * P:(k % 4 + 1) * P],
                                    h_rows[:, t, k * P:(k + 1) * P], ident[:, :])
                    last.then_inc(hT_ps, 1)

            def project(chunks, arrived, used, source, finished, kept):
                with pe.Fori(0, chunks) as c:
                    for i in range(2):
                        pe.wait_ge(arrived[i], 16 * c + 16)
                        for t in range(TB):
                            if i == 0:
                                pe.wait_ge(kept[t], c)
                            for k in range(8):
                                last = mm(ps[:, t, :], source[:, 8 * i + k, t * P:(t + 1) * P], w_half[i][:, k, :],
                                          start=(i == 0 and k == 0), stop=(i == 1 and k == 7))
                            if i == 1:
                                last.then_inc(finished[t], 1)
                        if i == 0:
                            last.then_inc(used, 1)

            pe.wait_ge(const_step, 6)
            pe.wait_ge(vec_in, 16 * 10)
            turn(ps[:, 3, 0:N_VEC], vec_rows[:, :], ident[0:N_VEC, 0:N_VEC]).then_inc(vec_ps, 1)
            norm(0)
            pe.wait_ge(hT_by_act, 2 * TB)
            pe.wait_ge(hT_by_dve, 2 * TB)
            pe.wait_ge(vec_ready, 1)
            project(3 * ATTN // CHUNK, w_in_half, w_half0_used, hT, proj_done, proj_kept)
            for t in range(TB):
                pe.wait_ge(proj_kept[t], 3 * ATTN // CHUNK)

            with pe.Fori(0, HEADS) as j:
                def conv(s, bank, k0, k1):
                    for k in range(k0, k1):
                        last = mm(ps[:, bank, :], w_conv[s][:, k, :], hT[:, k, :], start=(k == 0), stop=(k == KT - 1))
                    if k1 == KT:
                        last.then_inc(conv_done[s], 1)

                def scores(qb):
                    pe.wait_ge(scores_read[qb % 2], 4 * j + 2 * (qb // 2))
                    for c in range(2):
                        last = mm(ps[:, 2 + 2 * (qb % 2) + c, 0:(qb + 1) * P],
                                  qkT[c * HD:(c + 1) * HD, 0, qb * P:(qb + 1) * P],
                                  qkT[c * HD:(c + 1) * HD, 1, 0:(qb + 1) * P], start=True, stop=True)
                    last.then_inc(scores_done, 1)

                def turn_a(qb):
                    pe.wait_ge(a_ready, TB * j + qb + 1)
                    pe.wait_ge(aT_ready, TB * j + qb)
                    for kb in range(qb + 1):
                        last = turn(ps[:, 6, kb * P:(kb + 1) * P], probs[:, qb % 2, 0, kb * P:(kb + 1) * P],
                                    ident[:, :])
                    last.then_inc(a_turned[qb % 2], 1)

                def apply_v(qb):
                    pe.wait_ge(aT_ready, TB * j + qb + 1)
                    for kb in range(qb + 1):
                        last = mm(ps[:, 7, qb * P:(qb + 1) * P], aT[:, qb % 2, kb * P:(kb + 1) * P],
                                  qkv[:, kb, bass.ds(j * P + 2 * ATTN, P)], start=(kb == 0), stop=(kb == qb))
                    last.then_inc(av_done[qb % 2], 1)

                pe.wait_ge(cw_in[0], 16 * j + 16)
                pe.wait_ge(conv_gated, j)
                conv(0, 0, 0, KT)
                for i in range(2):
                    pe.wait_ge(qk_normed, 2 * j + i + 1)
                    if i == 0:
                        pe.wait_ge(o_out, j)
                    else:
                        pe.wait_ge(o_normed, j)
                    for t in range(TB):
                        last = turn(ps[:, 6 + i, t * P:(t + 1) * P], qk_n[:, i, t * P:(t + 1) * P], ident[:, :])
                    last.then_inc(qkT_ps, 1)
                pe.wait_ge(cw_in[1], 16 * j + 16)
                pe.wait_ge(c_kept, j)
                conv(1, 1, 0, 4)
                pe.wait_ge(qkT_ready, 2 * j + 2)
                scores(0)
                scores(1)
                conv(1, 1, 4, 10)
                turn_a(0)
                scores(2)
                conv(1, 1, 10, KT)
                apply_v(0)
                turn_a(1)
                scores(3)
                pe.wait_ge(cw_in[2], 16 * j + 16)
                pe.wait_ge(b_kept, j + 1)
                conv(2, 0, 0, 5)
                apply_v(1)
                turn_a(2)
                conv(2, 0, 5, 10)
                apply_v(2)
                turn_a(3)
                conv(2, 0, 10, 13)
                apply_v(3)
                conv(2, 0, 13, KT)
                pe.wait_ge(o_normed, j + 1)
                for t in range(TB):
                    last = turn(ps[:, 6, t * P:(t + 1) * P], o_n[:, t * P:(t + 1) * P], ident[:, :])
                last.then_inc(oT_ps, 1)
            pe.wait_ge(o_out, HEADS)
            pe.wait_ge(conv_out, HEADS)
            project(D // CHUNK, wo_half, wo_half0_used, mixT, out_done, out_added)
            norm(1)
            pe.wait_ge(hT_by_act, 4 * TB)
            pe.wait_ge(hT_by_dve, 4 * TB)

            def query_tile(h, k):
                if k == 0:
                    pe.wait_ge(wq_in, 16 * h + 16)
                    pe.wait_ge(keysT_ready, h)
                for c in range(2):
                    last = mm(ps_pq[:, c, :], w_peer[:, k, c * HALF:(c + 1) * HALF], hT[:, k, :],
                              start=(k == 0), stop=(k == KT - 1))
                if k == KT - 1:
                    last.then_inc(wq_used, 1)

            def key_scoring(h):
                pe.wait_ge(keys_in, 16 * h + 16)
                pe.wait_ge(pqT_ready, h + 1)
                for c in range(2):
                    last = turn(ps_keysT[:, c, :], keys[:, c, :], ident[:, :])
                last.then_inc(keys_used, 1)
                pe.wait_ge(keysT_ready, h + 1)
                pe.wait_ge(key_scores_ready, h)
                for c in range(2):
                    for t in range(TB):
                        last = mm(ps_key_scores[:, c, t, :], pqT[:, c, t * P:(t + 1) * P], keysT[:, c, :],
                                  start=True, stop=True)
                last.then_inc(key_scores_ps, 1)

            def head(h, last):
                for t in range(TB):
                    unit = TB * h + t
                    if t == 1 and not last:
                        key_scoring(h + 1)
                    pe.wait_ge(diag_ready, unit + 1)
                    pe.wait_ge(rows_added, unit)
                    for s in range(TOPK):
                        pe.wait_ge(v_in[s % RING], 16 * (4 * unit + s // RING + 1))
                        for n in range(D // CHUNK):
                            added = mm(ps[:, n, :], diag[:, s, :], v_rows[s % RING][:, n * CHUNK:(n + 1) * CHUNK],
                                       start=(s == 0), stop=(s == TOPK - 1))
                        added.then_inc(v_used[s % RING], 1)
                        if t == 0 and not last:
                            query_tile(h + 1, s)

            for k in range(KT):
                query_tile(0, k)
            key_scoring(0)
            with pe.Fori(0, PEER_HEADS - 1) as h:
                head(h, last=False)
            head(PEER_HEADS - 1, last=True)


_INS = ["x", "attn_norm_g", "w_in", "q_norm_g", "k_norm_g", "lambda_q1", "lambda_k1", "lambda_q2", "lambda_k2",
        "subln_g", "conv_w", "w_out", "ffn_norm_g", "peer_w_q", "peer_subkeys", "peer_u", "peer_v"]


def kernel(**inputs):
    import numpy as _np
    import concourse.bacc as _bacc
    from concourse.bass_utils import run_bass_kernel_spmd as _run

    nc = _bacc.Bacc("TRN2", target_bir_lowering=False, num_devices=1)
    arrays, args = {}, []
    for name in _INS:
        a = _np.ascontiguousarray(inputs[name])
        arrays[f"in_{name}"] = a
        args.append(nc.dram_tensor(f"in_{name}", a.shape, mybir.dt.from_np(a.dtype), kind="ExternalInput").ap())
    args.append(nc.dram_tensor("out", (1, SEQ, D), F32, kind="ExternalOutput").ap())
    decoder_layer(nc, *args)
    return _run(nc, [arrays], core_ids=[0]).results[0]["out"]
```

```python
from contextlib import ExitStack
import math

import concourse.bass as bass
from concourse import mybir

F32 = mybir.dt.float32
F32R = mybir.dt.float32r
U32 = mybir.dt.uint32
ALU = mybir.AluOpType
ACT = mybir.ActivationFunctionType
AX = mybir.AxisListType

P = 128
SEQ = 512
D = 2048
KT = D // P
TB = SEQ // P
ATTN = D // 2
CONV = D - ATTN
HEADS = 8
HD = 64
VD = 2 * HD
CT = CONV // P
TAPS = 3
CHUNK = 512
PEER_HEADS = 8
N_KEYS = 128
N_EXPERTS = N_KEYS * N_KEYS
HALF = 128
TOPK = 16
SWEPT = SEQ - P
SWEPT_BLOCKS = TB - 1
TILES = N_EXPERTS // P
GROUP = 8
RING = 8
EPS = 1e-6
LAM_INIT = 0.8 - 0.6 * math.exp(-0.3 * 0)
MASKED = -1.0e30
LOWEST = -3.0e38

V_Q, V_K, V_SUB, V_CONV = 0, 1, 2, 3
N_VEC = V_CONV + TAPS * CT

assert CT == HEADS and VD == P and HALF == P and N_KEYS == P
assert TILES == PEER_HEADS * TOPK


class Steps:

    def __init__(self, engine, sem):
        self.engine, self.sem, self.base, self.n = engine, sem, 0, 0

    def done(self, instruction):
        instruction.then_inc(self.sem, 1)
        self.n += 1
        return self.base + self.n

    def link(self, instruction):
        self.engine.wait_ge(self.sem, self.done(instruction))

    def enter(self, i, per):
        self.outside, self.first, self.per = self.base, self.n, per
        self.base = self.base + i * per

    def leave(self, trips):
        assert self.n - self.first == self.per, f"{self.n - self.first} steps, not {self.per}"
        self.base = self.outside + (trips - 1) * self.per


def decoder_layer(nc, x, attn_norm_g, w_in, q_norm_g, k_norm_g, lambda_q1, lambda_k1, lambda_q2, lambda_k2,
                  subln_g, conv_w, w_out, ffn_norm_g, peer_w_q, peer_subkeys, peer_u, peer_v, out):
    ctx = ExitStack()
    with ctx:
        def sb(name, shape, dt=F32):
            return ctx.enter_context(nc.sbuf_tensor(name, shape, dt))

        def sem(name):
            return ctx.enter_context(nc.semaphore(name))

        def sems(name, n):
            return [sem(f"{name}{i}") for i in range(n)]

        x_v = x[0].rearrange("(t p) d -> t p d", p=P)
        out_v = out[0].rearrange("(t p) d -> t p d", p=P)
        w_in_v = w_in[0].rearrange("(k p) n -> p k n", p=P)
        w_out_v = w_out[0].rearrange("(k p) n -> p k n", p=P)
        w_q_v = peer_w_q[0].rearrange("(k p) n -> p k n", p=P)
        subkeys_v = peer_subkeys[0].rearrange("h c k d -> k (h c) d")
        u_table, v_table = peer_u[0], peer_v[0]

        KB = 1024
        base = -(-nc.sbuf_base // 64) * 64
        sb("arena", [P, (184 * KB + 64) // 4])
        assert nc.sbuf_base >= base + 184 * KB

        def at(name, kb, shape, dt=F32):
            return nc.alloc_sbuf_tensor_at(name, shape, dt, offset=base + int(kb * KB))

        hT = at("hT", 0, [P, KT, SEQ])
        h2T_hi = at("h2T_hi", 0, [P, KT, SEQ], F32R)
        w_half = [at(f"w_half{i}", 32 + 16 * i, [P, 8, CHUNK]) for i in range(2)]
        w_conv = [at(f"w_conv{i}", 32 + 8 * i, [P, KT, P]) for i in range(3)]
        wq_hi = at("wq_hi", 32, [P, KT, 2 * HALF], F32R)
        wq_lo = at("wq_lo", 48, [P, KT, 2 * HALF], F32R)
        u_tile = [at(f"u_tile{i}", 32 + 8 * i, [P, D]) for i in range(2)]
        uT_hi = [at(f"uT_hi{i}", 48 + 4 * i, [P, 8, P], F32R) for i in range(2)]
        uT_lo = [at(f"uT_lo{i}", 56 + 4 * i, [P, 8, P], F32R) for i in range(2)]
        qkv = at("qkv", 64, [P, TB, 3 * ATTN])
        x_rows = at("x_rows", 64, [P, TB, D])
        w_peer = at("w_peer", 96, [P, KT, 2 * HALF])
        u_row1 = at("u_row1", 96, [P, D])
        products = [at(f"products{i}", 104 + 1.5 * i, [P, SWEPT]) for i in range(2)]
        h_rows = at("h_rows", 112, [P, TB, D])
        mixT = at("mixT", 112, [P, KT, SEQ])
        pqT = at("pqT", 120, [P, 2, SEQ])
        key_scores = at("key_scores", 124, [P, 2, TB, N_KEYS])
        keys = at("keys", 128, [P, 2, HALF])
        keysT = at("keysT", 129, [P, 2, N_KEYS])
        v_row = [at(f"v_row{i}", 120 + 8 * i, [P, D]) for i in range(2)]
        u_row = [at("u_row0", 136, [P, D]), u_row1]
        squares = [at("squares", 144, [P, D]), at("squares2", 96, [P, D])]
        qk_n = at("qk_n", 144, [P, 2, SEQ])
        sq = at("sq", 148, [P, 2, SEQ])
        conv_u, conv_y = at("conv_u", 148, [P, SEQ])[:, :], at("conv_y", 150, [P, SEQ])[:, :]
        qkT = at("qkT", 152, [P, 2, SEQ])
        probs = at("probs", 156, [P, 2, 2, SEQ])
        aT = at("aT", 164, [P, 2, SEQ])
        o_sq, o_n = at("o_sq", 168, [P, SEQ])[:, :], at("o_n", 170, [P, SEQ])[:, :]
        b_sb, c_sb = at("b_sb", 172, [P, SEQ])[:, :], at("c_sb", 174, [P, SEQ])[:, :]
        h2T_lo = at("h2T_lo", 144, [P, KT, SEQ], F32R)
        v_ring = [at(f"v_ring{i}", 8 * i, [P, D]) for i in range(RING)]
        gain = at("gain", 176, [P, D])[:, :]
        diag = at("diag", 176, [P, 4, 3, P])

        ident = sb("ident", [P, P])
        iota16 = sb("iota16", [P, TOPK])
        token_col = sb("token_col", [P, SWEPT_BLOCKS])
        alibi = sb("alibi", [P, SEQ])
        vec_rows = sb("vec_rows", [N_VEC, P])
        vec = sb("vec", [P, N_VEC])
        lam_in = sb("lam_in", [P, 4, HD])
        lam_prod = sb("lam_prod", [P, HD])
        lam = sb("lam", [P, 4])
        neg_lam = sb("neg_lam", [P, 1])
        ssq = sb("ssq", [P, 2 * TB])
        rstd = sb("rstd", [P, 2 * TB])
        qk_ss = sb("qk_ss", [P, 16])
        minus_half = sb("minus_half", [P, 16])
        conv_taps = sb("conv_taps", [P, TAPS, 1])
        row_max = sb("row_max", [P, 2, 2])
        neg_max = sb("neg_max", [P, 2, 2])
        row_sum = sb("row_sum", [P, 2, 2])
        inv_sum = sb("inv_sum", [P, 2, 2])
        o_ss = sb("o_ss", [P, TB])
        rest = sb("rest", [P, N_KEYS])
        half_top = sb("half_top", [P, 2, TOPK])
        half_idx = sb("half_idx", [P, 2, TOPK], U32)
        half_num = sb("half_num", [P, 2, TOPK])
        cand = sb("cand", [P, TOPK, TOPK])
        cand_rest = sb("cand_rest", [P, TOPK * TOPK])
        top = sb("top", [P, TB, TOPK])
        top_idx = sb("top_idx", [P, TOPK], U32)
        pair = sb("pair", [P, 2, TOPK], U32)
        pair_num = sb("pair_num", [P, 2, TOPK])
        pick = sb("pick", [P, 2, TOPK, TOPK])
        picked = sb("picked", [P, 2, TOPK])
        neg_top = sb("neg_top", [P, TB])
        gate_exps = sb("gate_exps", [P, TB, TOPK])
        gate_sum = sb("gate_sum", [P, TB])
        gate_inv = sb("gate_inv", [P, TB])
        experts = sb("experts", [P, TB, PEER_HEADS * TOPK], U32)
        gates = sb("gates", [P, TB, PEER_HEADS * TOPK])
        cells = sb("cells", [P, SWEPT_BLOCKS, PEER_HEADS * TOPK], U32)
        experts0 = sb("experts0", [P, 2, GROUP // 2], U32)
        experts_at = sb("experts_at", [P, SWEPT_BLOCKS, TOPK], U32)
        cells_at = sb("cells_at", [P, SWEPT_BLOCKS, TOPK], U32)
        dots0 = sb("dots0", [P, GROUP])
        gelus0 = sb("gelus0", [P, GROUP])
        acts0 = sb("acts0", [P, GROUP])
        dots = sb("dots", [P, TOPK])
        gelus = sb("gelus", [P, TOPK])
        acts = sb("acts", [P, TOPK])

        products_all = nc.dram_tensor("products_all", (N_EXPERTS * SWEPT, 1), F32, kind="Internal").ap()
        products_v = products_all.rearrange("(e t) o -> e (t o)", t=SWEPT)

        ps = ctx.enter_context(nc.psum_tensor("ps", [P, 8, CHUNK], F32))
        ps_rows = ps[:, 0:TB, :].rearrange("p b n -> p (b n)")
        ps_pq = ps[:, 4:6, :]
        ps_keysT = ps[:, 4, 0:2 * P].rearrange("p (c n) -> p c n", c=2)
        ps_key_scores = ps[:, 6:8, :].rearrange("p c (t n) -> p c t n", t=TB)
        ps_uT = [ps[:, 2 * i:2 * i + 2, :].rearrange("p b (k e) -> p (b k) e", k=4) for i in range(2)]

        const_step = sem("const_step")
        x_in = sems("x_in", TB)
        gain_in = sem("gain_in")
        vec_in = sem("vec_in")
        vec_ps = sem("vec_ps")
        vec_ready = sem("vec_ready")
        lam_sum = sem("lam_sum")
        lam_exp = sem("lam_exp")
        ssq_ready = sem("ssq_ready")
        mean_ready = sem("mean_ready")
        rstd_ready = sem("rstd_ready")
        qk_mean = sem("qk_mean")
        qk_rstd = sem("qk_rstd")
        o_mean = sem("o_mean")
        o_rstd = sem("o_rstd")
        h_ready = sem("h_ready")
        hT_ps = sem("hT_ps")
        hT_by_act = sem("hT_by_act")
        hT_by_dve = sem("hT_by_dve")
        h2T_hi_ready = sem("h2T_hi_ready")
        h2T_ready = sem("h2T_ready")
        w_in_half = sems("w_in_half", 2)
        w_half0_used = sem("w_half0_used")
        proj_done = sems("proj_done", TB)
        proj_kept = sems("proj_kept", TB)
        cw_in = sems("cw_in", 3)
        conv_done = sems("conv_done", 3)
        b_kept = sem("b_kept")
        c_kept = sem("c_kept")
        conv_gated = sem("conv_gated")
        conv_out = sem("conv_out")
        qk_normed = sem("qk_normed")
        qkT_ps = sem("qkT_ps")
        qkT_ready = sem("qkT_ready")
        scores_done = sem("scores_done")
        scores_read = sems("scores_read", 2)
        max_ready = sem("max_ready")
        exp_done = sem("exp_done")
        a_ready = sem("a_ready")
        a_turned = sems("a_turned", 2)
        aT_ready = sem("aT_ready")
        av_done = sems("av_done", 2)
        o_squared = sem("o_squared")
        o_normed = sem("o_normed")
        oT_ps = sem("oT_ps")
        o_out = sem("o_out")
        wo_half = sems("wo_half", 2)
        wo_half0_used = sem("wo_half0_used")
        out_done = sems("out_done", TB)
        out_added = sems("out_added", TB)
        wq_in = sem("wq_in")
        wq_used = sem("wq_used")
        keys_in = sem("keys_in")
        keys_used = sem("keys_used")
        pqT_ready = sem("pqT_ready")
        keysT_ready = sem("keysT_ready")
        key_scores_ps = sem("key_scores_ps")
        key_scores_ready = sem("key_scores_ready")
        key_scores_read = sem("key_scores_read")
        wq_hi_ready = sem("wq_hi_ready")
        wq_ready = sem("wq_ready")
        chosen = sem("chosen")
        top_ready = sem("top_ready")
        gates_exp = sem("gates_exp")
        cells_ready = sem("cells_ready")
        staged0 = sem("staged0")
        staged = sem("staged")
        u_tile_in = sems("u_tile_in", 2)
        uT_half0_ps = sem("uT_half0_ps")
        uT_half1_ps = sems("uT_half1_ps", 2)
        uT_hi_ready = sems("uT_hi_ready", 2)
        uT_ready = sems("uT_ready", 2)
        swept = sems("swept", 2)
        swept_kept = sems("swept_kept", 2)
        swept_stored = sems("swept_stored", 2)
        u_in = sems("u_in", 2)
        u_used = sems("u_used", 2)
        v0_in = sems("v0_in", 2)
        v0_used = sems("v0_used", 2)
        gelu0_done = sem("gelu0_done")
        cells_in = sem("cells_in")
        v_in = sems("v_in", RING)
        v_used = sems("v_used", RING)
        gelu_done = sem("gelu_done")
        acts_ready = sem("acts_ready")
        diag_ready = sem("diag_ready")
        rows_added = sem("rows_added")
        out_stored = sem("out_stored")
        dve_step = sem("dve_step")
        act_step = sem("act_step")
        pool_past = sem("pool_past")
        dve_past = sem("dve_past")
        nc_block = ctx.enter_context(nc.Block())

        @nc_block.sync
        def _(sp):
            for t in range(TB):
                sp.dma_start(x_rows[:, t, :], x_v[t]).then_inc(x_in[t], 16)
                if t == 0:
                    sp.dma_start(gain, attn_norm_g[0:1, :].to_broadcast([P, D])).then_inc(gain_in, 16)
            with sp.Fori(0, 3 * ATTN // CHUNK) as c:
                for i in range(2):
                    sp.wait_ge(w_half0_used if i == 0 else proj_done[TB - 1], c)
                    sp.dma_start(w_half[i][:, :, :], w_in_v[:, 8 * i:8 * i + 8, bass.ds(c * CHUNK, CHUNK)])\
                        .then_inc(w_in_half[i], 16)
            sp.wait_ge(w_half0_used, 3 * ATTN // CHUNK)
            sp.wait_ge(proj_done[TB - 1], 3 * ATTN // CHUNK)
            with sp.Fori(0, CT) as j:
                for s in range(3):
                    sp.wait_ge(conv_done[s], j)
                    sp.dma_start(w_conv[s][:, :, :], w_in_v[:, :, bass.ds(j * P + (3 * ATTN + s * CONV), P)])\
                        .then_inc(cw_in[s], 16)
            sp.wait_ge(h_ready, TB)
            sp.dma_start(gain, ffn_norm_g[0:1, :].to_broadcast([P, D])).then_inc(gain_in, 16)
            sp.wait_ge(av_done[1], 2 * HEADS)
            sp.wait_ge(qk_normed, 2 * HEADS)
            for t in range(TB):
                sp.dma_start(x_rows[:, t, :], x_v[t]).then_inc(x_in[t], 16)
            for s in range(3):
                sp.wait_ge(conv_done[s], CT)
            with sp.Fori(0, D // CHUNK) as c:
                for i in range(2):
                    sp.wait_ge(wo_half0_used if i == 0 else out_done[TB - 1], c)
                    sp.dma_start(w_half[i][:, :, :], w_out_v[:, 8 * i:8 * i + 8, bass.ds(c * CHUNK, CHUNK)])\
                        .then_inc(wo_half[i], 16)
            sp.wait_ge(ssq_ready, 2 * TB)
            sp.wait_ge(hT_ps, 2 * TB)
            with sp.Fori(0, PEER_HEADS) as h:
                sp.wait_ge(wq_ready, h)
                sp.dma_start(w_peer[:, :, :], w_q_v[:, :, bass.ds(h * 2 * HALF, 2 * HALF)]).then_inc(wq_in, 16)
                sp.wait_ge(keys_used, h)
                sp.dma_start(keys[:, :, :], subkeys_v[:, bass.ds(h * 2, 2), :]).then_inc(keys_in, 16)
            sp.wait_ge(wq_used, PEER_HEADS)
            with sp.Fori(0, TILES // 2) as i:
                for b in range(2):
                    sp.wait_ge(uT_half1_ps[b], i)
                    sp.dma_start(u_tile[b][:, :], u_table[bass.ds(i * 2 * P + b * P, P), :])\
                        .then_inc(u_tile_in[b], 16)
            sp.wait_ge(v0_used[1], TILES // 2)
            sp.dma_start(out_v[0], x_rows[:, 0, :]).then_inc(out_stored, 16)
            for t in range(1, TB):
                sp.wait_ge(rows_added, (PEER_HEADS - 1) * SWEPT_BLOCKS + t)
                sp.dma_start(out_v[t], x_rows[:, t, :]).then_inc(out_stored, 16)
            sp.wait_ge(out_stored, 16 * TB)

        @nc_block.gpsimd
        def _(pool):
            pool.memset(ident[:, :], 0.0).then_inc(const_step, 1)
            pool.iota(iota16[:, :], [[1, TOPK]], base=0, channel_multiplier=0,
                      allow_small_or_imprecise_dtypes=True).then_inc(const_step, 1)
            pool.iota(alibi[:, :], [[1, SEQ]], base=-(SEQ - P), channel_multiplier=-1,
                      allow_small_or_imprecise_dtypes=True).then_inc(const_step, 1)
            pool.iota(token_col[:, :], [[P, SWEPT_BLOCKS]], base=0, channel_multiplier=1,
                      allow_small_or_imprecise_dtypes=True).then_inc(const_step, 1)
            pool.memset(minus_half[:, :], -0.5).then_inc(const_step, 1)
            pool.wait_ge(const_step, 5)
            pool.affine_select(out=ident[:, :], in_=ident[:, :], compare_op=ALU.not_equal, fill=1.0,
                               base=0, pattern=[[-1, P]], channel_multiplier=1).then_inc(const_step, 1)
            pool.affine_select(out=alibi[:, :], in_=alibi[:, :], compare_op=ALU.is_ge, fill=MASKED,
                               base=SEQ - P, pattern=[[-1, SEQ]], channel_multiplier=1).then_inc(const_step, 1)
            for i, row in ((0, q_norm_g), (1, k_norm_g)):
                for c in range(2):
                    pool.dma_start(vec_rows[i:i + 1, c * HD:(c + 1) * HD], row[0:1, :]).then_inc(vec_in, 16)
            pool.dma_start(vec_rows[V_SUB:V_SUB + 1, :], subln_g[0:1, :]).then_inc(vec_in, 16)
            pool.dma_start(vec_rows[V_CONV:N_VEC, :], conv_w[0].rearrange("j (c p) -> (j c) p", p=P))\
                .then_inc(vec_in, 16)
            for i, row in enumerate((lambda_q1, lambda_k1, lambda_q2, lambda_k2)):
                pool.dma_start(lam_in[:, i, :], row[0:1, :].to_broadcast([P, HD])).then_inc(vec_in, 16)

            def inverse_root(a):
                return nc.gpsimd.tensor_tensor(a, a, minus_half[:, 0:a.shape[1]], ALU.pow)

            def norm(n):
                for i in range(n * TB, (n + 1) * TB):
                    pool.wait_ge(mean_ready, i + 1)
                    inverse_root(rstd[:, i:i + 1]).then_inc(rstd_ready, 1)

            norm(0)
            with pool.Fori(0, HEADS) as j:
                pool.wait_ge(qk_mean, j + 1)
                inverse_root(qk_ss[:, :]).then_inc(qk_rstd, 1)
                pool.wait_ge(o_mean, j + 1)
                inverse_root(o_ss[:, :]).then_inc(o_rstd, 1)
            norm(1)

            pool.wait_ge(chosen, TB * PEER_HEADS)
            pool.wait_ge(wq_used, PEER_HEADS)
            pool.wait_ge(key_scores_read, TB * PEER_HEADS)
            with pool.Fori(0, TILES // GROUP) as i:
                for b in range(GROUP):
                    which, col = divmod(b, GROUP // 2)
                    if col == 0:
                        nc.gpsimd.tensor_copy(experts0[:, which, :], experts[:, 0, bass.ds(i * GROUP + b, GROUP // 2)])\
                            .then_inc(staged0, 1)
                        pool.wait_ge(staged0, 2 * i + which + 1)
                        pool.sem_inc(pool_past, 1)
                    index = bass.IndirectOffsetOnAxis(ap=experts0[:, which, col:col + 1], axis=0)
                    pool.wait_ge(u_used[b % 2], GROUP // 2 * i + b // 2)
                    pool.sem_inc(pool_past, 1)
                    pool.indirect_dma_start(out=u_row[b % 2][:, :], out_offset=None, in_=u_table,
                                            in_offset=index).then_inc(u_in[b % 2], 16)
                    pool.wait_ge(v0_used[b % 2], GROUP // 2 * i + b // 2)
                    pool.sem_inc(pool_past, 1)
                    pool.indirect_dma_start(out=v_row[b % 2][:, :], out_offset=None, in_=v_table,
                                            in_offset=index).then_inc(v0_in[b % 2], 16)

            def stage(n, h, t):
                cols = slice(h * TOPK, (h + 1) * TOPK) if isinstance(h, int) else bass.ds(h * TOPK, TOPK)
                nc.gpsimd.tensor_copy(experts_at[:, t - 1, :], experts[:, t, cols]).then_inc(staged, 1)
                nc.gpsimd.tensor_copy(cells_at[:, t - 1, :], cells[:, t - 1, cols]).then_inc(staged, 1)
                pool.wait_ge(staged, 2 * n + 2)
                pool.sem_inc(pool_past, 1)

            def fetch_product(t, s):
                pool.indirect_dma_start(
                    out=dots[:, s:s + 1], out_offset=None, in_=products_all,
                    in_offset=bass.IndirectOffsetOnAxis(ap=cells_at[:, t - 1, s:s + 1], axis=0))\
                    .then_inc(cells_in, 16)

            def gather_v(n, t, s):
                pool.wait_ge(v_used[s % RING], TOPK // RING * n + s // RING)
                pool.sem_inc(pool_past, 1)
                pool.indirect_dma_start(
                    out=v_ring[s % RING][:, :], out_offset=None, in_=v_table,
                    in_offset=bass.IndirectOffsetOnAxis(ap=experts_at[:, t - 1, s:s + 1], axis=0))\
                    .then_inc(v_in[s % RING], 16)

            def head(h, last):
                for t in range(1, TB):
                    n = SWEPT_BLOCKS * h + t - 1
                    ahead = not (last and t == TB - 1)
                    if ahead:
                        pool.wait_ge(gelu_done, n + 1)
                        pool.sem_inc(pool_past, 1)
                    for s in range(TOPK):
                        gather_v(n, t, s)
                        if ahead:
                            fetch_product(t % SWEPT_BLOCKS + 1, s)
                    if t == 1:
                        stage(n + 2, h, 3)
                    elif not last:
                        stage(n + 2, h + 1, t - 1)

            pool.wait_ge(cells_ready, 1)
            stage(0, 0, 1)
            stage(1, 0, 2)
            for b in range(2):
                pool.wait_ge(swept_stored[b], 16 * TILES // 2)
                pool.wait_ge(swept[b], TILES // 2)
            for s in range(TOPK):
                fetch_product(1, s)
            with pool.Fori(0, PEER_HEADS - 1) as h:
                head(h, last=False)
            head(PEER_HEADS - 1, last=True)

        @nc_block.scalar
        def _(act):
            steps = Steps(act, act_step)

            def norm(n):
                for t in range(TB + 1):
                    if t < TB:
                        if n == 0:
                            act.wait_ge(x_in[t], 16)
                        else:
                            act.wait_ge(out_added[t], D // CHUNK)
                        if n * TB + t > 0:
                            act.wait_ge(ssq_ready, n * TB + t)
                        nc.scalar.activation(squares[n][:, :], x_rows[:, t, :], ACT.Square,
                                             accum_out=ssq[:, n * TB + t:n * TB + t + 1]).then_inc(ssq_ready, 1)
                    if t > 0:
                        act.wait_ge(hT_ps, n * TB + t)
                        for b in range(2 if n == 0 else 4):
                            nc.scalar.activation((hT if n == 0 else h2T_hi)[:, 4 * b:4 * b + 4, (t - 1) * P:t * P],
                                                 ps[:, 4 + b, :].rearrange("p (k t) -> p k t", k=4),
                                                 ACT.Copy).then_inc(hT_by_act if n == 0 else h2T_hi_ready, 1)

            act.wait_ge(lam_sum, 1)
            nc.scalar.activation(lam[:, 2:4], lam[:, 0:2], ACT.Exp).then_inc(lam_exp, 1)
            norm(0)
            with act.Fori(0, 3 * ATTN // CHUNK) as c:
                for t in (0, 2):
                    act.wait_ge(proj_done[t], c + 1)
                    nc.scalar.activation(qkv[:, t, bass.ds(c * CHUNK, CHUNK)], ps[:, t, :], ACT.Copy)\
                        .then_inc(proj_kept[t], 1)
            act.wait_ge(vec_ready, 1)
            with act.Fori(0, HEADS) as j:
                def exps(qb):
                    act.wait_ge(max_ready, TB * j + qb + 1)
                    for c in range(2):
                        part = probs[:, qb % 2, c, 0:(qb + 1) * P]
                        nc.scalar.activation(part, part, ACT.Exp, bias=neg_max[:, qb % 2, c:c + 1],
                                             accum_out=row_sum[:, qb % 2, c:c + 1]).then_inc(exp_done, 1)

                def keep_aT(qb):
                    act.wait_ge(a_turned[qb % 2], 2 * j + qb // 2 + 1)
                    act.wait_ge(av_done[qb % 2], 2 * j + qb // 2)
                    nc.scalar.activation(aT[:, qb % 2, 0:(qb + 1) * P], ps[:, 6, 0:(qb + 1) * P], ACT.Copy)\
                        .then_inc(aT_ready, 1)

                act.wait_ge(conv_done[0], j + 1)
                act.wait_ge(conv_out, j)
                nc.scalar.activation(b_sb, ps[:, 0, :], ACT.Copy).then_inc(b_kept, 1)
                for i in range(2):
                    act.wait_ge(qkT_ps, 2 * j + i + 1)
                    nc.scalar.activation(qkT[:, i, :], ps[:, 6 + i, :], ACT.Copy,
                                         scale=vec[:, V_Q + i:V_Q + i + 1]).then_inc(qkT_ready, 1)
                exps(0)
                exps(1)
                keep_aT(0)
                exps(2)
                act.wait_ge(conv_done[1], j + 1)
                act.wait_ge(conv_gated, j)
                nc.scalar.activation(c_sb, ps[:, 1, :], ACT.Copy).then_inc(c_kept, 1)
                keep_aT(1)
                exps(3)
                keep_aT(2)
                keep_aT(3)
                act.wait_ge(av_done[1], 2 * j + 2)
                nc.scalar.activation(o_sq, ps[:, 7, :], ACT.Square).then_inc(o_squared, 1)
                act.wait_ge(oT_ps, j + 1)
                nc.scalar.activation(mixT[:, bass.ds(j, 1), :], ps[:, 6:7, :], ACT.Copy,
                                     scale=vec[:, V_SUB:V_SUB + 1]).then_inc(o_out, 1)
            norm(1)

            def split_wq(h):
                act.wait_ge(wq_in, 16 * h + 16)
                act.wait_ge(wq_used, h)
                nc.scalar.activation(wq_hi[:, :, :], w_peer[:, :, :], ACT.Copy).then_inc(wq_hi_ready, 1)

            def choice(h, last):
                act.wait_ge(wq_used, h + 1)
                nc.scalar.activation(pqT[:, :, :], ps_pq, ACT.Copy).then_inc(pqT_ready, 1)
                if not last:
                    split_wq(h + 1)
                act.wait_ge(keys_used, h + 1)
                nc.scalar.activation(keysT[:, :, :], ps_keysT, ACT.Copy).then_inc(keysT_ready, 1)
                act.wait_ge(key_scores_ps, h + 1)
                act.wait_ge(key_scores_read, TB * h)
                nc.scalar.activation(key_scores[:, :, :, :], ps_key_scores, ACT.Copy)\
                    .then_inc(key_scores_ready, 1)
                for t in range(TB):
                    act.wait_ge(top_ready, TB * h + t + 1)
                    nc.scalar.activation(gate_exps[:, t, :], top[:, t, :], ACT.Exp, bias=neg_top[:, t:t + 1],
                                         accum_out=gate_sum[:, t:t + 1]).then_inc(gates_exp, 1)

            split_wq(0)
            with act.Fori(0, PEER_HEADS - 1) as h:
                choice(h, last=False)
            choice(PEER_HEADS - 1, last=True)

            def split_u(i, b, half):
                if half == 0:
                    act.wait_ge(uT_half0_ps, GROUP * i + b + 1)
                else:
                    act.wait_ge(uT_half1_ps[b % 2], GROUP // 2 * i + b // 2 + 1)
                nc.scalar.activation(uT_hi[half][:, :, :], ps_uT[half], ACT.Copy).then_inc(uT_hi_ready[half], 1)

            def sweep(i, last):
                for b in range(GROUP):
                    c = GROUP * i + b
                    act.wait_ge(u_used[b % 2], GROUP // 2 * i + b // 2 + 1)
                    nc.scalar.activation(gelus0[:, b:b + 1], dots0[:, b:b + 1], ACT.Gelu).then_inc(gelu0_done, 1)
                    if not (last and b == GROUP - 1):
                        split_u(i, b + 1, 0)
                    act.wait_ge(swept[b % 2], GROUP // 2 * i + b // 2 + 1)
                    act.wait_ge(swept_stored[b % 2], 16 * (GROUP // 2 * i + b // 2))
                    nc.scalar.activation(products[b % 2][:, :], ps[:, 4 + b % 2, 0:SWEPT], ACT.Copy)\
                        .then_inc(swept_kept[b % 2], 1)
                    act.wait_ge(swept_kept[b % 2], GROUP // 2 * i + b // 2 + 1)
                    act.dma_start(products_v[bass.ds(i * GROUP * P + b * P, P), :] if not last else
                                  products_v[c * P:(c + 1) * P, :], products[b % 2][:, :])\
                        .then_inc(swept_stored[b % 2], 16)
                    if not (last and b == GROUP - 1):
                        split_u(i, b + 1, 1)

            split_u(0, 0, 0)
            split_u(0, 0, 1)
            with act.Fori(0, TILES // GROUP - 1) as i:
                sweep(i, last=False)
            sweep(TILES // GROUP - 1, last=True)

            def gelu(n):
                act.wait_ge(cells_in, 16 * TOPK * (n + 1))
                act.wait_ge(acts_ready, n)
                nc.scalar.activation(gelus[:, :], dots[:, :], ACT.Gelu).then_inc(gelu_done, 1)

            with act.Fori(0, PEER_HEADS * SWEPT_BLOCKS) as n:
                gelu(n)

        @nc_block.vector
        def _(dve):
            v = nc.vector
            steps = Steps(dve, dve_step)
            link, done = steps.link, steps.done

            def past():
                dve.sem_inc(dve_past, 1)

            def norm(n):
                for t in range(TB + 1):
                    i = n * TB + t
                    if t < TB:
                        dve.wait_ge(ssq_ready, i + 1)
                        v.tensor_scalar(rstd[:, i:i + 1], ssq[:, i:i + 1], 1.0 / D, EPS, ALU.mult, ALU.add)\
                            .then_inc(mean_ready, 1)
                        dve.wait_ge(rstd_ready, i + 1)
                        if t == 0:
                            dve.wait_ge(gain_in, 16 * (n + 1))
                        v.scalar_tensor_tensor(out=h_rows[:, t, :], in0=x_rows[:, t, :], scalar=rstd[:, i:i + 1],
                                               in1=gain, op0=ALU.mult, op1=ALU.mult).then_inc(h_ready, 1)
                    if t > 0:
                        dve.wait_ge(hT_ps, i)
                        for b in range(2, 4) if n == 0 else range(4):
                            bank = ps[:, 4 + b, :].rearrange("p (k t) -> p k t", k=4)
                            part = slice(4 * b, 4 * b + 4), slice((t - 1) * P, t * P)
                            if n == 0:
                                v.tensor_copy(hT[:, *part], bank).then_inc(hT_by_dve, 1)
                            else:
                                dve.wait_ge(h2T_hi_ready, 4 * (t - 1) + b + 1)
                                v.tensor_tensor(h2T_lo[:, *part], bank, h2T_hi[:, *part].bitcast(F32), ALU.subtract)\
                                    .then_inc(h2T_ready, 1)

            dve.wait_ge(vec_in, 16 * 10)
            for i in range(2):
                link(v.tensor_tensor(lam_prod[:, :], lam_in[:, 2 * i, :], lam_in[:, 2 * i + 1, :], ALU.mult))
                ins = v.reduce_sum(lam[:, i:i + 1], lam_prod[:, :], axis=AX.X)
                if i == 0:
                    link(ins)
                else:
                    ins.then_inc(lam_sum, 1)
            dve.wait_ge(vec_ps, 1)
            link(v.tensor_copy(vec[:, :], ps[:, 3, 0:N_VEC]))
            link(v.tensor_scalar(vec[:, V_Q:V_Q + 1], vec[:, V_Q:V_Q + 1], HD ** -0.5, None, ALU.mult))
            v.tensor_scalar(vec[:, V_SUB:V_SUB + 1], vec[:, V_SUB:V_SUB + 1], 1.0 - LAM_INIT, None, ALU.mult)\
                .then_inc(vec_ready, 1)
            dve.wait_ge(lam_exp, 1)
            link(v.tensor_tensor(neg_lam[:, :], lam[:, 3:4], lam[:, 2:3], ALU.subtract))
            link(v.tensor_scalar(neg_lam[:, :], neg_lam[:, :], -LAM_INIT, None, ALU.add))
            norm(0)
            with dve.Fori(0, 3 * ATTN // CHUNK) as c:
                for t in (1, 3):
                    dve.wait_ge(proj_done[t], c + 1)
                    v.tensor_copy(qkv[:, t, bass.ds(c * CHUNK, CHUNK)], ps[:, t, :]).then_inc(proj_kept[t], 1)
            for t in range(TB):
                dve.wait_ge(proj_kept[t], 3 * ATTN // CHUNK)

            per_head = 21
            with dve.Fori(0, HEADS) as j:
                steps.enter(j, per_head)
                dve.wait_ge(qkT_ps, 2 * j)
                rows = [qkv[:, :, bass.ds(i * ATTN + j * P, P)] for i in range(2)]
                done(v.tensor_tensor(sq[:, 0, :].rearrange("p (t n) -> p t n", t=TB), rows[0], rows[0], ALU.mult))
                link(v.tensor_tensor(sq[:, 1, :].rearrange("p (t n) -> p t n", t=TB), rows[1], rows[1], ALU.mult))
                link(v.reduce_sum(qk_ss[:, :], sq[:, :, :].rearrange("p a (g d) -> p (a g) d", d=HD), axis=AX.X))
                v.tensor_scalar(qk_ss[:, :], qk_ss[:, :], 1.0 / HD, EPS, ALU.mult, ALU.add).then_inc(qk_mean, 1)
                dve.wait_ge(qk_rstd, j + 1)
                for i in range(2):
                    v.tensor_tensor(qk_n[:, i, :].rearrange("p (t c d) -> p t c d", t=TB, c=2),
                                    rows[i].rearrange("p t (c d) -> p t c d", c=2),
                                    qk_ss[:, 8 * i:8 * i + 8].rearrange("p (t c) -> p t c", c=2).unsqueeze(3)
                                    .to_broadcast([P, TB, 2, HD]), ALU.mult).then_inc(qk_normed, 1)
                done(v.tensor_scalar(alibi[:, :], alibi[:, :], 0.5, None, ALU.mult))
                link(v.tensor_copy(conv_taps[:, :, :],
                                   vec[:, V_CONV:N_VEC].rearrange("p (a c) -> p a c", a=TAPS)[:, :, bass.ds(j, 1)]))

                def biased(qb):
                    n = (qb + 1) * P
                    dve.wait_ge(scores_done, TB * j + qb + 1)
                    dve.wait_ge(a_turned[qb % 2], 2 * j + qb // 2)
                    past()
                    for c in range(2):
                        v.tensor_tensor_reduce(out=probs[:, qb % 2, c, 0:n], in0=ps[:, 2 + 2 * (qb % 2) + c, 0:n],
                                               in1=alibi[:, SEQ - n:SEQ], scale=1.0, scalar=LOWEST,
                                               op0=ALU.add, op1=ALU.max, accum_out=row_max[:, qb % 2, c:c + 1])\
                            .then_inc(scores_read[qb % 2], 1)
                    dve.wait_ge(scores_read[qb % 2], 4 * j + 2 * (qb // 2) + 2)
                    v.tensor_scalar(neg_max[:, qb % 2, :], row_max[:, qb % 2, :], -1.0, None, ALU.mult)\
                        .then_inc(max_ready, 1)

                def combined(qb):
                    n, i = (qb + 1) * P, qb % 2
                    dve.wait_ge(exp_done, 2 * (TB * j + qb) + 2)
                    link(v.reciprocal(inv_sum[:, i, :], row_sum[:, i, :]))
                    link(v.tensor_tensor(inv_sum[:, i, 1:2], inv_sum[:, i, 1:2], neg_lam[:, :], ALU.mult))
                    link(v.tensor_scalar(probs[:, i, 1, 0:n], probs[:, i, 1, 0:n], inv_sum[:, i, 1:2], None, ALU.mult))
                    past()
                    v.scalar_tensor_tensor(out=probs[:, i, 0, 0:n], in0=probs[:, i, 0, 0:n],
                                           scalar=inv_sum[:, i, 0:1], in1=probs[:, i, 1, 0:n],
                                           op0=ALU.mult, op1=ALU.add).then_inc(a_ready, 1)

                biased(0)
                biased(1)
                combined(0)
                biased(2)
                combined(1)
                biased(3)
                combined(2)
                combined(3)
                dve.wait_ge(o_squared, j + 1)
                link(v.reduce_sum(o_ss[:, :], o_sq.rearrange("p (t n) -> p t n", t=TB), axis=AX.X))
                v.tensor_scalar(o_ss[:, :], o_ss[:, :], 1.0 / VD, EPS, ALU.mult, ALU.add).then_inc(o_mean, 1)
                dve.wait_ge(o_rstd, j + 1)
                dve.wait_ge(oT_ps, j)
                v.tensor_tensor(o_n.rearrange("p (t n) -> p t n", t=TB),
                                ps[:, 7, :].rearrange("p (t n) -> p t n", t=TB),
                                o_ss[:, :].unsqueeze(2).to_broadcast([P, TB, VD]), ALU.mult).then_inc(o_normed, 1)
                dve.wait_ge(c_kept, j + 1)
                dve.wait_ge(conv_done[2], j + 1)
                v.tensor_tensor(conv_u, ps[:, 0, :], c_sb, ALU.mult).then_inc(conv_gated, 1)
                dve.wait_ge(conv_gated, j + 1)
                link(v.tensor_scalar(conv_y, conv_u, conv_taps[:, 2, :], None, ALU.mult))
                for lag in (1, 2):
                    past()
                    link(v.scalar_tensor_tensor(out=conv_y[:, lag:], in0=conv_u[:, 0:SEQ - lag],
                                                scalar=conv_taps[:, 2 - lag, :], in1=conv_y[:, lag:],
                                                op0=ALU.mult, op1=ALU.add))
                dve.wait_ge(b_kept, j + 1)
                v.tensor_tensor(mixT[:, bass.ds(j + HEADS, 1), :].squeeze(1), conv_y, b_sb, ALU.mult)\
                    .then_inc(conv_out, 1)
                dve.wait_ge(conv_out, j + 1)
                steps.leave(HEADS)
            for t in range(TB):
                dve.wait_ge(x_in[t], 32)
            with dve.Fori(0, D // CHUNK) as c:
                for t in range(TB):
                    part = x_rows[:, t, bass.ds(c * CHUNK, CHUNK)]
                    dve.wait_ge(out_done[t], c + 1)
                    v.tensor_tensor(part, ps[:, t, :], part, ALU.add).then_inc(out_added[t], 1)
            norm(1)

            def top16(values, indices, source, remains):
                past()
                link(v.max(values[:, 0:8], source))
                past()
                done(v.max_index(indices[:, 0:8], values[:, 0:8], source))
                link(v.match_replace(remains, values[:, 0:8], source, LOWEST))
                past()
                link(v.max(values[:, 8:16], remains))
                past()
                link(v.max_index(indices[:, 8:16], values[:, 8:16], remains))

            def choose_half(t, c):
                top16(half_top[:, c, :], half_idx[:, c, :], key_scores[:, c, t, :], rest[:, :])

            def choose_pairs(unit, t):
                v.tensor_scalar(half_num[:, 0, :], half_idx[:, 0, :], float(N_KEYS), None, ALU.mult)\
                    .then_inc(key_scores_read, 1)
                done(v.tensor_copy(half_num[:, 1, :], half_idx[:, 1, :]))
                link(v.tensor_tensor(cand[:, :, :],
                                     half_top[:, 0, :].unsqueeze(2).to_broadcast([P, TOPK, TOPK]),
                                     half_top[:, 1, :].unsqueeze(1).to_broadcast([P, TOPK, TOPK]), ALU.add))
                top16(top[:, t, :], top_idx, cand[:, :, :].rearrange("p a b -> p (a b)"), cand_rest[:, :])
                v.tensor_scalar(neg_top[:, t:t + 1], top[:, t, 0:1], -1.0, None, ALU.mult).then_inc(top_ready, 1)

            def choose_experts(unit, t, cols):
                done(v.tensor_scalar(pair[:, 0, :], top_idx[:, :], 4, None, ALU.logical_shift_right))
                link(v.tensor_scalar(pair[:, 1, :], top_idx[:, :], TOPK - 1, None, ALU.bitwise_and))
                link(v.tensor_copy(pair_num[:, :, :], pair[:, :, :]))
                link(v.tensor_tensor(pick[:, :, :, :].rearrange("p c s a -> p (c s) a"),
                                     pair_num[:, :, :].rearrange("p c s -> p (c s)").unsqueeze(2)
                                     .to_broadcast([P, 2 * TOPK, TOPK]),
                                     iota16[:, :].unsqueeze(1).to_broadcast([P, 2 * TOPK, TOPK]), ALU.is_equal))
                dve.wait_ge(key_scores_read, unit + 1)
                link(v.tensor_tensor(pick[:, :, :, :], pick[:, :, :, :],
                                     half_num[:, :, :].unsqueeze(2).to_broadcast([P, 2, TOPK, TOPK]), ALU.mult))
                link(v.reduce_sum(picked[:, :, :].rearrange("p c s -> p (c s)"),
                                  pick[:, :, :, :].rearrange("p c s a -> p (c s) a"), axis=AX.X))
                v.tensor_tensor(experts[:, t, cols], picked[:, 0, :], picked[:, 1, :], ALU.add)\
                    .then_inc(chosen, 1)

            def split_wq(h):
                dve.wait_ge(wq_hi_ready, h + 1)
                v.tensor_tensor(wq_lo[:, :, :], w_peer[:, :, :], wq_hi[:, :, :].bitcast(F32), ALU.subtract)\
                    .then_inc(wq_ready, 1)

            def choice(h, last):
                cols = slice(h * TOPK, (h + 1) * TOPK) if last else bass.ds(h * TOPK, TOPK)
                if not last:
                    split_wq(h + 1)
                dve.wait_ge(key_scores_ready, h + 1)
                for t in range(TB):
                    choose_half(t, 0)
                    choose_half(t, 1)
                    choose_pairs(TB * h + t, t)
                    choose_experts(TB * h + t, t, cols)
                dve.wait_ge(gates_exp, TB * h + TB)
                link(v.reciprocal(gate_inv[:, :], gate_sum[:, :]))
                link(v.tensor_tensor(gates[:, :, cols], gate_exps[:, :, :],
                                     gate_inv[:, :].unsqueeze(2).to_broadcast([P, TB, TOPK]), ALU.mult))

            split_wq(0)
            with dve.Fori(0, PEER_HEADS - 1) as h:
                steps.enter(h, 94)
                choice(h, last=False)
                steps.leave(PEER_HEADS - 1)
            choice(PEER_HEADS - 1, last=True)
            dve.wait_ge(chosen, TB * PEER_HEADS)
            for t in range(1, TB):
                ins = v.tensor_scalar(cells[:, t - 1, :], experts[:, t, :], float(SWEPT), token_col[:, t - 1:t],
                                      ALU.mult, ALU.add)
                if t < TB - 1:
                    done(ins)
                else:
                    ins.then_inc(cells_ready, 1)

            def split_u(c, half):
                dve.wait_ge(uT_hi_ready[half], c + 1)
                v.tensor_tensor(uT_lo[half][:, :, :], ps_uT[half], uT_hi[half][:, :, :].bitcast(F32), ALU.subtract)\
                    .then_inc(uT_ready[half], 1)

            def sweep(i, last):
                for b in range(GROUP):
                    c = GROUP * i + b
                    use = GROUP // 2 * i + b // 2 + 1
                    dve.wait_ge(u_in[b % 2], 16 * use)
                    v.tensor_tensor_reduce(out=u_row[b % 2][:, :], in0=u_row[b % 2][:, :], in1=h_rows[:, 0, :],
                                           scale=1.0, scalar=0.0, op0=ALU.mult, op1=ALU.add,
                                           accum_out=dots0[:, b:b + 1]).then_inc(u_used[b % 2], 1)
                    if not (last and b == GROUP - 1):
                        split_u(c + 1, 0)
                    dve.wait_ge(gelu0_done, c + 1)
                    gate = gates[:, 0, c:c + 1] if last else gates[:, 0, bass.ds(i * GROUP + b, 1)]
                    link(v.tensor_tensor(acts0[:, b:b + 1], gelus0[:, b:b + 1], gate, ALU.mult))
                    dve.wait_ge(v0_in[b % 2], 16 * use)
                    past()
                    v.scalar_tensor_tensor(out=x_rows[:, 0, :], in0=v_row[b % 2][:, :], scalar=acts0[:, b:b + 1],
                                           in1=x_rows[:, 0, :], op0=ALU.mult, op1=ALU.add)\
                        .then_inc(v0_used[b % 2], 1)
                    if not (last and b == GROUP - 1):
                        split_u(c + 1, 1)
                    dve.wait_ge(v0_used[b % 2], use)

            split_u(0, 0)
            split_u(0, 1)
            with dve.Fori(0, TILES // GROUP - 1) as i:
                steps.enter(i, GROUP)
                sweep(i, last=False)
                steps.leave(TILES // GROUP - 1)
            sweep(TILES // GROUP - 1, last=True)

            def weigh(n, h, t):
                cols = slice(h * TOPK, (h + 1) * TOPK) if isinstance(h, int) else bass.ds(h * TOPK, TOPK)
                dve.wait_ge(gelu_done, n + 1)
                v.tensor_tensor(acts[:, :], gelus[:, :], gates[:, t, cols], ALU.mult).then_inc(acts_ready, 1)
                dve.wait_ge(acts_ready, n + 1)

            def spread():
                v.tensor_tensor(diag[:, :, :, :],
                                ident[:, :].unsqueeze(1).unsqueeze(1).to_broadcast([P, 4, 3, P]),
                                acts[:, :].rearrange("p (a b) -> p a b", b=4)[:, :, 0:3].unsqueeze(3)
                                .to_broadcast([P, 4, 3, P]), ALU.mult).then_inc(diag_ready, 1)

            def head(h, last):
                for t in range(1, TB):
                    n = SWEPT_BLOCKS * h + t - 1
                    for s in range(3, TOPK, 4):
                        use = TOPK // RING * n + s // RING + 1
                        dve.wait_ge(v_in[s % RING], 16 * use)
                        past()
                        v.scalar_tensor_tensor(out=x_rows[:, t, :], in0=v_ring[s % RING][:, :],
                                               scalar=acts[:, s:s + 1], in1=x_rows[:, t, :],
                                               op0=ALU.mult, op1=ALU.add).then_inc(v_used[s % RING], 1)
                        dve.wait_ge(v_used[s % RING], use)
                    if not (last and t == TB - 1):
                        weigh(n + 1, h if t < TB - 1 else h + 1, t % SWEPT_BLOCKS + 1)
                    dve.wait_ge(v_used[(TOPK - 2) % RING], TOPK // RING * (n + 1))
                    v.tensor_tensor(x_rows[:, t, :], ps_rows, x_rows[:, t, :], ALU.add).then_inc(rows_added, 1)
                    if not (last and t == TB - 1):
                        spread()

            weigh(0, 0, 1)
            spread()
            with dve.Fori(0, PEER_HEADS - 1) as h:
                head(h, last=False)
            head(PEER_HEADS - 1, last=True)

        @nc_block.tensor
        def _(pe):
            mm, turn = nc.tensor.matmul, nc.tensor.transpose

            def norm(n):
                for t in range(TB):
                    pe.wait_ge(h_ready, n * TB + t + 1)
                    if n == 0 and t > 0:
                        pe.wait_ge(hT_by_act, 2 * t)
                        pe.wait_ge(hT_by_dve, 2 * t)
                    if n == 1 and t > 0:
                        pe.wait_ge(h2T_ready, 4 * t)
                    for k in range(KT):
                        last = turn(ps[:, 4 + k // 4, (k % 4) * P:(k % 4 + 1) * P],
                                    h_rows[:, t, k * P:(k + 1) * P], ident[:, :])
                    last.then_inc(hT_ps, 1)

            def project(chunks, arrived, used, source, finished, kept):
                with pe.Fori(0, chunks) as c:
                    for i in range(2):
                        pe.wait_ge(arrived[i], 16 * c + 16)
                        for t in range(TB):
                            if i == 0:
                                pe.wait_ge(kept[t], c)
                            for k in range(8):
                                last = mm(ps[:, t, :], source[:, 8 * i + k, t * P:(t + 1) * P], w_half[i][:, k, :],
                                          start=(i == 0 and k == 0), stop=(i == 1 and k == 7))
                            if i == 1:
                                last.then_inc(finished[t], 1)
                        if i == 0:
                            last.then_inc(used, 1)

            pe.wait_ge(const_step, 7)
            pe.wait_ge(vec_in, 16 * 10)
            turn(ps[:, 3, 0:N_VEC], vec_rows[:, :], ident[0:N_VEC, 0:N_VEC]).then_inc(vec_ps, 1)
            norm(0)
            pe.wait_ge(hT_by_act, 2 * TB)
            pe.wait_ge(hT_by_dve, 2 * TB)
            pe.wait_ge(vec_ready, 1)
            project(3 * ATTN // CHUNK, w_in_half, w_half0_used, hT, proj_done, proj_kept)
            for t in range(TB):
                pe.wait_ge(proj_kept[t], 3 * ATTN // CHUNK)

            with pe.Fori(0, HEADS) as j:
                def conv(s, bank, k0, k1):
                    for k in range(k0, k1):
                        last = mm(ps[:, bank, :], w_conv[s][:, k, :], hT[:, k, :], start=(k == 0), stop=(k == KT - 1))
                    if k1 == KT:
                        last.then_inc(conv_done[s], 1)

                def scores(qb):
                    pe.wait_ge(scores_read[qb % 2], 4 * j + 2 * (qb // 2))
                    for c in range(2):
                        last = mm(ps[:, 2 + 2 * (qb % 2) + c, 0:(qb + 1) * P],
                                  qkT[c * HD:(c + 1) * HD, 0, qb * P:(qb + 1) * P],
                                  qkT[c * HD:(c + 1) * HD, 1, 0:(qb + 1) * P], start=True, stop=True)
                    last.then_inc(scores_done, 1)

                def turn_a(qb):
                    pe.wait_ge(a_ready, TB * j + qb + 1)
                    pe.wait_ge(aT_ready, TB * j + qb)
                    for kb in range(qb + 1):
                        last = turn(ps[:, 6, kb * P:(kb + 1) * P], probs[:, qb % 2, 0, kb * P:(kb + 1) * P],
                                    ident[:, :])
                    last.then_inc(a_turned[qb % 2], 1)

                def apply_v(qb):
                    pe.wait_ge(aT_ready, TB * j + qb + 1)
                    for kb in range(qb + 1):
                        last = mm(ps[:, 7, qb * P:(qb + 1) * P], aT[:, qb % 2, kb * P:(kb + 1) * P],
                                  qkv[:, kb, bass.ds(j * P + 2 * ATTN, P)], start=(kb == 0), stop=(kb == qb))
                    last.then_inc(av_done[qb % 2], 1)

                pe.wait_ge(cw_in[0], 16 * j + 16)
                pe.wait_ge(conv_gated, j)
                conv(0, 0, 0, KT)
                for i in range(2):
                    pe.wait_ge(qk_normed, 2 * j + i + 1)
                    if i == 0:
                        pe.wait_ge(o_out, j)
                    else:
                        pe.wait_ge(o_normed, j)
                    for t in range(TB):
                        last = turn(ps[:, 6 + i, t * P:(t + 1) * P], qk_n[:, i, t * P:(t + 1) * P], ident[:, :])
                    last.then_inc(qkT_ps, 1)
                pe.wait_ge(cw_in[1], 16 * j + 16)
                pe.wait_ge(c_kept, j)
                conv(1, 1, 0, 4)
                pe.wait_ge(qkT_ready, 2 * j + 2)
                scores(0)
                scores(1)
                conv(1, 1, 4, 10)
                turn_a(0)
                scores(2)
                conv(1, 1, 10, KT)
                apply_v(0)
                turn_a(1)
                scores(3)
                pe.wait_ge(cw_in[2], 16 * j + 16)
                pe.wait_ge(b_kept, j + 1)
                conv(2, 0, 0, 5)
                apply_v(1)
                turn_a(2)
                conv(2, 0, 5, 10)
                apply_v(2)
                turn_a(3)
                conv(2, 0, 10, 13)
                apply_v(3)
                conv(2, 0, 13, KT)
                pe.wait_ge(o_normed, j + 1)
                for t in range(TB):
                    last = turn(ps[:, 6, t * P:(t + 1) * P], o_n[:, t * P:(t + 1) * P], ident[:, :])
                last.then_inc(oT_ps, 1)
            pe.wait_ge(o_out, HEADS)
            pe.wait_ge(conv_out, HEADS)
            project(D // CHUNK, wo_half, wo_half0_used, mixT, out_done, out_added)
            norm(1)
            pe.wait_ge(h2T_ready, 4 * TB)

            def split_products(out, w_hi, w_lo, m_hi, m_lo, first, last):
                mm(out, w_hi, m_hi, start=first, stop=False)
                mm(out, w_lo, m_hi, start=False, stop=False)
                return mm(out, w_hi, m_lo, start=False, stop=last)

            with pe.Fori(0, PEER_HEADS) as h:
                pe.wait_ge(wq_ready, h + 1)
                pe.wait_ge(keysT_ready, h)
                pe.wait_ge(pqT_ready, h)
                for k in range(KT):
                    for c in range(2):
                        cols = slice(c * HALF, (c + 1) * HALF)
                        last = split_products(ps_pq[:, c, :], wq_hi[:, k, cols], wq_lo[:, k, cols],
                                              h2T_hi[:, k, :], h2T_lo[:, k, :], k == 0, k == KT - 1)
                last.then_inc(wq_used, 1)
                pe.wait_ge(keys_in, 16 * h + 16)
                pe.wait_ge(pqT_ready, h + 1)
                for c in range(2):
                    last = turn(ps_keysT[:, c, :], keys[:, c, :], ident[:, :])
                last.then_inc(keys_used, 1)
                pe.wait_ge(keysT_ready, h + 1)
                pe.wait_ge(key_scores_ready, h)
                for c in range(2):
                    for t in range(TB):
                        last = mm(ps_key_scores[:, c, t, :], pqT[:, c, t * P:(t + 1) * P], keysT[:, c, :],
                                  start=True, stop=True)
                last.then_inc(key_scores_ps, 1)

            def turned(buffer, use, half):
                if half == 0:
                    pe.wait_ge(u_tile_in[buffer], 16 * use)
                for k in range(8):
                    last = turn(ps_uT[half][:, k, :], u_tile[buffer][:, (8 * half + k) * P:(8 * half + k + 1) * P],
                                ident[:, :])
                last.then_inc(uT_half0_ps if half == 0 else uT_half1_ps[buffer], 1)

            def sweep(i, last):
                for b in range(GROUP):
                    c = GROUP * i + b
                    more = not (last and b == GROUP - 1)
                    nxt = (b + 1) % 2
                    for half in range(2):
                        pe.wait_ge(uT_ready[half], c + 1)
                        if half == 0:
                            pe.wait_ge(swept_kept[b % 2], GROUP // 2 * i + b // 2)
                        for k in range(8):
                            summed = split_products(ps[:, 4 + b % 2, 0:SWEPT], uT_hi[half][:, k, :],
                                                    uT_lo[half][:, k, :], h2T_hi[:, 8 * half + k, P:SEQ],
                                                    h2T_lo[:, 8 * half + k, P:SEQ],
                                                    half == 0 and k == 0, half == 1 and k == 7)
                        if half == 1:
                            summed.then_inc(swept[b % 2], 1)
                        if more:
                            turned(nxt, GROUP // 2 * i + (b + 1) // 2 + 1, half)

            turned(0, 1, 0)
            turned(0, 1, 1)
            with pe.Fori(0, TILES // GROUP - 1) as i:
                sweep(i, last=False)
            sweep(TILES // GROUP - 1, last=True)

            def head(h, last):
                for t in range(1, TB):
                    n = SWEPT_BLOCKS * h + t - 1
                    pe.wait_ge(diag_ready, n + 1)
                    pe.wait_ge(rows_added, n)
                    for s in range(TOPK):
                        if s % 4 == 3:
                            continue
                        pe.wait_ge(v_in[s % RING], 16 * (TOPK // RING * n + s // RING + 1))
                        for m in range(D // CHUNK):
                            added = mm(ps[:, m, :], diag[:, s // 4, s % 4, :],
                                       v_ring[s % RING][:, m * CHUNK:(m + 1) * CHUNK],
                                       start=(s == 0), stop=(s == TOPK - 2))
                        added.then_inc(v_used[s % RING], 1)

            with pe.Fori(0, PEER_HEADS - 1) as h:
                head(h, last=False)
            head(PEER_HEADS - 1, last=True)


_INS = ["x", "attn_norm_g", "w_in", "q_norm_g", "k_norm_g", "lambda_q1", "lambda_k1", "lambda_q2", "lambda_k2",
        "subln_g", "conv_w", "w_out", "ffn_norm_g", "peer_w_q", "peer_subkeys", "peer_u", "peer_v"]


def kernel(**inputs):
    import numpy as _np
    import concourse.bacc as _bacc
    from concourse.bass_utils import run_bass_kernel_spmd as _run

    nc = _bacc.Bacc("TRN2", target_bir_lowering=False, num_devices=1)
    arrays, args = {}, []
    for name in _INS:
        a = _np.ascontiguousarray(inputs[name])
        arrays[f"in_{name}"] = a
        args.append(nc.dram_tensor(f"in_{name}", a.shape, mybir.dt.from_np(a.dtype), kind="ExternalInput").ap())
    args.append(nc.dram_tensor("out", (1, SEQ, D), F32, kind="ExternalOutput").ap())
    decoder_layer(nc, *args)
    return _run(nc, [arrays], core_ids=[0]).results[0]["out"]
```

```python
from contextlib import ExitStack
import math

import concourse.bass as bass
from concourse import mybir

F32 = mybir.dt.float32
F32R = mybir.dt.float32r
U32 = mybir.dt.uint32
ALU = mybir.AluOpType
ACT = mybir.ActivationFunctionType
AX = mybir.AxisListType

P = 128
SEQ = 512
D = 2048
KT = D // P
TB = SEQ // P
ATTN = D // 2
CONV = D - ATTN
HEADS = 8
HD = 64
VD = 2 * HD
CT = CONV // P
TAPS = 3
CHUNK = 512
PEER_HEADS = 8
N_KEYS = 128
N_EXPERTS = N_KEYS * N_KEYS
HALF = 128
TOPK = 16
SWEPT = SEQ - P
SWEPT_BLOCKS = TB - 1
TILES = N_EXPERTS // P
QUARTER = KT // 4
HALF_KT = KT // 2
PIECES = 6
PIECE_RING = 3
QKV_CHUNKS = 3 * ATTN // CHUNK
OUT_CHUNKS = D // CHUNK
MIX_ORDER = (0, 2, 1, 3)
RING = 8
EPS = 1e-6
LAM_INIT = 0.8 - 0.6 * math.exp(-0.3 * 0)
MASKED = -1.0e30
LOWEST = -3.0e38

V_Q, V_K, V_SUB, V_CONV = 0, 1, 2, 3
N_VEC = V_CONV + TAPS * CT

assert CT == HEADS and VD == P and HALF == P and N_KEYS == P
assert TILES == PEER_HEADS * TOPK

SPLIT_WQ = (1, 7)
QUERIES = (2, 8)
KEYS_TURNED = 6
QUERIES_OUT = (6, 12)
KEY_SCORES = (7, 13)
WQ_LOADS = (0, 5)


class Steps:

    def __init__(self, engine, sem):
        self.engine, self.sem, self.base, self.n = engine, sem, 0, 0

    def done(self, instruction):
        instruction.then_inc(self.sem, 1)
        self.n += 1
        return self.base + self.n

    def link(self, instruction):
        self.engine.wait_ge(self.sem, self.done(instruction))

    def enter(self, i, per):
        self.outside, self.first, self.per = self.base, self.n, per
        self.base = self.base + i * per

    def leave(self, trips):
        assert self.n - self.first == self.per, f"{self.n - self.first} steps, not {self.per}"
        self.base = self.outside + (trips - 1) * self.per


def decoder_layer(nc, x, attn_norm_g, w_in, q_norm_g, k_norm_g, lambda_q1, lambda_k1, lambda_q2, lambda_k2,
                  subln_g, conv_w, w_out, ffn_norm_g, peer_w_q, peer_subkeys, peer_u, peer_v, out):
    ctx = ExitStack()
    with ctx:
        def sb(name, shape, dt=F32):
            return ctx.enter_context(nc.sbuf_tensor(name, shape, dt))

        def sem(name):
            return ctx.enter_context(nc.semaphore(name))

        def sems(name, n):
            return [sem(f"{name}{i}") for i in range(n)]

        x_v = x[0].rearrange("(t p) d -> t p d", p=P)
        out_v = out[0].rearrange("(t p) d -> t p d", p=P)
        w_in_v = w_in[0].rearrange("(k p) n -> p k n", p=P)
        w_out_v = w_out[0].rearrange("(k p) n -> p k n", p=P)
        w_q_v = peer_w_q[0].rearrange("(k p) n -> p k n", p=P)
        subkeys_v = peer_subkeys[0].rearrange("h c k d -> k (h c) d")
        u_table, v_table = peer_u[0], peer_v[0]

        KB = 1024
        base = -(-nc.sbuf_base // 64) * 64
        sb("arena", [P, (184 * KB + 64) // 4])
        assert nc.sbuf_base >= base + 184 * KB

        def at(name, kb, shape, dt=F32):
            return nc.alloc_sbuf_tensor_at(name, shape, dt, offset=base + int(kb * KB))

        hT_hi = at("hT_hi", 0, [P, KT, SEQ], F32R)
        hT_lo = at("hT_lo", 32, [P, KT, SEQ], F32R)
        mix_hi, mix_lo, h2T_hi = hT_hi, hT_lo, hT_hi
        u_tile = [at(f"u_tile{i}", 32 + 8 * i, [P, D]) for i in range(2)]
        uT_hi = [at(f"uT_hi{i}", 48 + 4 * i, [P, 8, P], F32R) for i in range(2)]
        uT_lo = [at(f"uT_lo{i}", 56 + 4 * i, [P, 8, P], F32R) for i in range(2)]
        qkv = at("qkv", 64, [P, TB, 3 * ATTN])
        x_rows = at("x_rows", 64, [P, TB, D])
        squares = at("squares", 96, [P, D])
        w_peer0 = at("w_peer0", 32, [P, KT, HALF])
        wq0_hi = at("wq0_hi", 48, [P, KT, HALF], F32R)
        wq0_lo = at("wq0_lo", 56, [P, KT, HALF], F32R)
        w_peer = at("w_peer", 72, [P, KT, HALF])
        wq_hi = at("wq_hi", 80, [P, KT, HALF], F32R)
        wq_lo = at("wq_lo", 88, [P, KT, HALF], F32R)
        u_row1 = at("u_row1", 96, [P, D])
        products = [at(f"products{i}", 104 + 1.5 * i, [P, SWEPT]) for i in range(2)]
        h_rows = at("h_rows", 112, [P, TB, D])
        wi_lo = [at(f"wi_lo{i}", 112 + 8 * i, [P, QUARTER, CHUNK], F32R) for i in range(2)]
        wc_lo = at("wc_lo", 112, [P, PIECE_RING, HALF_KT, P], F32R)
        wc_hi = at("wc_hi", 128, [P, PIECE_RING, HALF_KT, P], F32R)
        mixT = at("mixT", 112, [P, KT, SEQ])
        wo_lo = [at(f"wo_lo{i}", 96 + 8 * i, [P, QUARTER, CHUNK], F32R) for i in range(2)]
        keys = at("keys", 107, [P, 2, HALF])
        keysT = at("keysT", 108, [P, 2, N_KEYS])
        v_row = [at(f"v_row{i}", 120 + 8 * i, [P, D]) for i in range(2)]
        u_row = [at("u_row0", 136, [P, D]), u_row1]
        w_hi = [at(f"w_hi{i}", 144 + 8 * i, [P, QUARTER, CHUNK], F32R) for i in range(2)]
        w_raw = [at(f"w_raw{i}", 160 + 8 * i, [P, QUARTER, CHUNK]) for i in range(2)]
        qk_n = at("qk_n", 144, [P, 2, SEQ])
        sq = at("sq", 148, [P, 2, SEQ])
        conv_u, conv_y = at("conv_u", 148, [P, SEQ])[:, :], at("conv_y", 150, [P, SEQ])[:, :]
        qkT = at("qkT", 152, [P, 2, SEQ])
        probs = at("probs", 156, [P, 2, 2, SEQ])
        aT = at("aT", 164, [P, 2, SEQ])
        o_mix = at("o_mix", 168, [P, SEQ])[:, :]
        o_sq, o_n = at("o_sq", 168, [P, SEQ])[:, :], at("o_n", 170, [P, SEQ])[:, :]
        b_sb, c_sb = at("b_sb", 172, [P, SEQ])[:, :], at("c_sb", 174, [P, SEQ])[:, :]
        h2T_lo = at("h2T_lo", 144, [P, KT, SEQ], F32R)
        v_ring = [at(f"v_ring{i}", (8 * i + 32) % 64, [P, D]) for i in range(RING)]
        gain = at("gain", 176, [P, D])[:, :]
        wc_raw = [at(f"wc_raw{i}", 176 + 4 * i, [P, HALF_KT, P]) for i in range(2)]
        pqT = at("pqT", 176, [P, 2, SEQ])
        key_scores = at("key_scores", 180, [P, 2, TB, N_KEYS])
        diag = at("diag", 176, [P, 4, 3, P])

        ident = sb("ident", [P, P])
        iota16 = sb("iota16", [P, TOPK])
        token_col = sb("token_col", [P, SWEPT_BLOCKS])
        alibi = sb("alibi", [P, SEQ])
        vec_rows = sb("vec_rows", [N_VEC, P])
        vec = sb("vec", [P, N_VEC])
        lam_in = sb("lam_in", [P, 4, HD])
        lam_prod = sb("lam_prod", [P, HD])
        lam = sb("lam", [P, 4])
        neg_lam = sb("neg_lam", [P, 1])
        ssq = sb("ssq", [P, 2 * TB])
        rstd = sb("rstd", [P, 2 * TB])
        qk_ss = sb("qk_ss", [P, 16])
        minus_half = sb("minus_half", [P, 16])
        conv_taps = sb("conv_taps", [P, TAPS, 1])
        row_max = sb("row_max", [P, 2, 2])
        neg_max = sb("neg_max", [P, 2, 2])
        row_sum = sb("row_sum", [P, 2, 2])
        inv_sum = sb("inv_sum", [P, 2, 2])
        o_ss = sb("o_ss", [P, TB])
        rest = sb("rest", [P, N_KEYS])
        half_top = sb("half_top", [P, 2, TOPK])
        half_idx = sb("half_idx", [P, 2, TOPK], U32)
        half_num = sb("half_num", [P, 2, TOPK])
        cand = sb("cand", [P, TOPK, TOPK])
        cand_rest = sb("cand_rest", [P, TOPK * TOPK])
        top = sb("top", [P, TB, TOPK])
        top_idx = sb("top_idx", [P, TOPK], U32)
        pair = sb("pair", [P, 2, TOPK], U32)
        pair_num = sb("pair_num", [P, 2, TOPK])
        pick = sb("pick", [P, 2, TOPK, TOPK])
        picked = sb("picked", [P, 2, TOPK])
        neg_top = sb("neg_top", [P, TB])
        gate_exps = sb("gate_exps", [P, TB, TOPK])
        gate_sum = sb("gate_sum", [P, TB])
        gate_inv = sb("gate_inv", [P, TB])
        experts = sb("experts", [P, TB, PEER_HEADS * TOPK], U32)
        gates = sb("gates", [P, TB, PEER_HEADS * TOPK])
        cells = sb("cells", [P, SWEPT_BLOCKS, PEER_HEADS * TOPK], U32)
        experts0 = sb("experts0", [P, 2, TOPK // 2], U32)
        experts_at = sb("experts_at", [P, SWEPT_BLOCKS, TOPK], U32)
        cells_at = sb("cells_at", [P, SWEPT_BLOCKS, TOPK], U32)
        dots0 = sb("dots0", [P, TOPK])
        gelus0 = sb("gelus0", [P, TOPK])
        acts0 = sb("acts0", [P, TOPK])
        dots = sb("dots", [P, TOPK])
        gelus = sb("gelus", [P, TOPK])
        acts = sb("acts", [P, TOPK])

        products_all = nc.dram_tensor("products_all", (N_EXPERTS * SWEPT, 1), F32, kind="Internal").ap()
        products_v = products_all.rearrange("(e t) o -> e (t o)", t=SWEPT)

        mix_all = nc.dram_tensor("mix_all", (KT, P, SEQ), F32, kind="Internal").ap()
        x_mid = nc.dram_tensor("x_mid", (SWEPT_BLOCKS, P, D), F32, kind="Internal").ap()

        ps = ctx.enter_context(nc.psum_tensor("ps", [P, 8, CHUNK], F32))
        ps_rows = ps[:, 0:TB, :].rearrange("p b n -> p (b n)")
        ps_pq = ps[:, 6, :]
        ps_keysT = ps[:, 7, 0:2 * P].rearrange("p (c n) -> p c n", c=2)
        ps_key_scores = [ps[:, 7 - c, :].rearrange("p (t n) -> p t n", t=TB) for c in range(2)]
        ps_uT = [ps[:, 2 * i:2 * i + 2, :].rearrange("p b (k e) -> p (b k) e", k=4) for i in range(2)]

        const_step = sem("const_step")
        x_in = sems("x_in", TB)
        gain_in = sem("gain_in")
        vec_in = sem("vec_in")
        vec_ps = sem("vec_ps")
        vec_ready = sem("vec_ready")
        lam_sum = sem("lam_sum")
        lam_exp = sem("lam_exp")
        ssq_ready = sem("ssq_ready")
        mean_ready = sem("mean_ready")
        rstd_ready = sem("rstd_ready")
        qk_mean = sem("qk_mean")
        qk_rstd = sem("qk_rstd")
        o_mean = sem("o_mean")
        o_rstd = sem("o_rstd")
        h_ready = sem("h_ready")
        hT_ps = sem("hT_ps")
        hT_hi_ready = sem("hT_hi_ready")
        hT_ready = sem("hT_ready")
        w_in_raw = sems("w_in_raw", 2)
        w_hi_ready = sem("w_hi_ready")
        w_ready = sem("w_ready")
        w_used = sems("w_used", 3)
        proj_done = sems("proj_done", TB)
        proj_kept = sems("proj_kept", TB)
        wc_in = sems("wc_in", 2)
        wc_hi_ready = sem("wc_hi_ready")
        wc_ready = sem("wc_ready")
        wc_half_used = sem("wc_half_used")
        conv_done = sems("conv_done", 3)
        b_kept = sem("b_kept")
        c_kept = sem("c_kept")
        conv_gated = sem("conv_gated")
        conv_out = sem("conv_out")
        qk_normed = sem("qk_normed")
        qkT_ps = sem("qkT_ps")
        qkT_ready = sem("qkT_ready")
        scores_done = sem("scores_done")
        scores_read = sems("scores_read", 2)
        max_ready = sem("max_ready")
        exp_done = sem("exp_done")
        a_ready = sem("a_ready")
        a_turned = sems("a_turned", 2)
        aT_ready = sem("aT_ready")
        av_done = sems("av_done", 2)
        o_squared = sem("o_squared")
        o_normed = sem("o_normed")
        oT_ps = sem("oT_ps")
        o_out = sem("o_out")
        o_stored = sem("o_stored")
        conv_stored = sem("conv_stored")
        mix_in = sems("mix_in", 4)
        mix_hi_ready = sem("mix_hi_ready")
        mix_ready = sem("mix_ready")
        out_done = sems("out_done", TB)
        out_added = sems("out_added", TB)
        x_mid_stored = sem("x_mid_stored")
        x_back = sem("x_back")
        wq_in = sems("wq_in", 2)
        wq_used = sem("wq_used")
        keys_in = sem("keys_in")
        keys_used = sem("keys_used")
        pqT_ready = sem("pqT_ready")
        keysT_ready = sem("keysT_ready")
        key_scores_ps = sem("key_scores_ps")
        key_scores_ready = sem("key_scores_ready")
        key_scores_read = sem("key_scores_read")
        wq_hi_ready = sem("wq_hi_ready")
        wq_ready = sem("wq_ready")
        chosen = sem("chosen")
        top_ready = sem("top_ready")
        gates_exp = sem("gates_exp")
        cells_ready = sem("cells_ready")
        staged0 = sem("staged0")
        staged = sem("staged")
        u_tile_in = sems("u_tile_in", 2)
        uT_half0_ps = sem("uT_half0_ps")
        uT_half1_ps = sems("uT_half1_ps", 2)
        uT_hi_ready = sems("uT_hi_ready", 2)
        uT_ready = sems("uT_ready", 2)
        swept = sems("swept", 2)
        swept_kept = sems("swept_kept", 2)
        swept_stored = sems("swept_stored", 2)
        u_in = sems("u_in", 2)
        u_used = sems("u_used", 2)
        v0_in = sems("v0_in", 2)
        v0_used = sems("v0_used", 2)
        gelu0_done = sem("gelu0_done")
        cells_in = sem("cells_in")
        v_in = sems("v_in", RING)
        v_used = sems("v_used", RING)
        gelu_done = sem("gelu_done")
        acts_ready = sem("acts_ready")
        diag_ready = sem("diag_ready")
        rows_added = sem("rows_added")
        out_stored = sem("out_stored")
        dve_step = sem("dve_step")
        act_step = sem("act_step")
        pool_past = sem("pool_past")
        dve_past = sem("dve_past")
        nc_block = ctx.enter_context(nc.Block())

        @nc_block.sync
        def _(sp):
            for t in range(TB):
                sp.dma_start(x_rows[:, t, :], x_v[t]).then_inc(x_in[t], 16)
                if t == 0:
                    sp.dma_start(gain, attn_norm_g[0:1, :].to_broadcast([P, D])).then_inc(gain_in, 16)

            def load_quarter(weights, c, q, order):
                rows = slice(QUARTER * order[q], QUARTER * (order[q] + 1))
                sp.dma_start(w_raw[q % 2][:, :, :],
                             weights[:, rows, bass.ds(c * CHUNK, CHUNK)])\
                    .then_inc(w_in_raw[q % 2], 16)

            def load_weights(chunks, weights, before, order=range(4)):
                with sp.Fori(0, chunks - 1) as c:
                    for q in range(4):
                        sp.wait_ge(w_ready, 4 * (c + before) + q + 1)
                        load_quarter(weights, c if q < 2 else c + 1, (q + 2) % 4, order)
                for q in range(2):
                    sp.wait_ge(w_ready, 4 * (before + chunks - 1) + q + 1)
                    load_quarter(weights, chunks - 1, q + 2, order)

            load_quarter(w_in_v, 0, 0, range(4))
            load_quarter(w_in_v, 0, 1, range(4))
            load_weights(QKV_CHUNKS, w_in_v, 0)

            def conv_piece(j, p):
                column = j * P + (3 * ATTN + p // 2 * CONV)
                sp.dma_start(wc_raw[p % 2][:, :, :],
                             w_in_v[:, HALF_KT * (p % 2):HALF_KT * (p % 2 + 1), bass.ds(column, P)])\
                    .then_inc(wc_in[p % 2], 16)

            sp.wait_ge(h_ready, TB)
            conv_piece(0, 0)
            conv_piece(0, 1)
            with sp.Fori(0, CT - 1) as j:
                for p in range(PIECES):
                    sp.wait_ge(wc_ready, PIECES * j + p + 1)
                    conv_piece(j + (p + 2) // PIECES, (p + 2) % PIECES)
            for p in range(PIECES - 2):
                sp.wait_ge(wc_ready, PIECES * (CT - 1) + p + 1)
                conv_piece(CT - 1, p + 2)
            sp.wait_ge(av_done[1], 2 * HEADS)
            load_quarter(w_out_v, 0, 0, MIX_ORDER)
            sp.wait_ge(wc_half_used, PIECES // 2 * CT)
            sp.wait_ge(o_stored, 16 * (HEADS - 1))
            sp.wait_ge(conv_stored, 16 * (HEADS - 1))
            for n, q in enumerate(MIX_ORDER):
                if n == 2:
                    sp.wait_ge(o_stored, 16 * HEADS)
                    sp.wait_ge(conv_stored, 16 * HEADS)
                    load_quarter(w_out_v, 0, 1, MIX_ORDER)
                sp.dma_start(mixT[:, QUARTER * q:QUARTER * (q + 1), :],
                             mix_all[QUARTER * q:QUARTER * (q + 1)].rearrange("k p t -> p k t")).then_inc(mix_in[q], 16)
            load_weights(OUT_CHUNKS, w_out_v, QKV_CHUNKS, MIX_ORDER)
            sp.wait_ge(out_done[TB - 1], OUT_CHUNKS)
            sp.wait_ge(out_done[0], OUT_CHUNKS)
            sp.dma_start(w_peer0[:, :, :], w_q_v[:, :, 0:HALF]).then_inc(wq_in[0], 16)
            sp.wait_ge(ssq_ready, 2 * TB)
            sp.wait_ge(hT_ps, 2 * TB)
            sp.dma_start(keys[:, :, :], subkeys_v[:, 0:2, :]).then_inc(keys_in, 16)
            for t in range(1, TB):
                sp.dma_start(x_mid[t - 1], x_rows[:, t, :]).then_inc(x_mid_stored, 16)
            sp.wait_ge(x_mid_stored, 16 * SWEPT_BLOCKS)
            sp.wait_ge(h_ready, 2 * TB)

            def load_wq(h, c):
                sp.wait_ge(wq_ready, 2 * h + c)
                sp.dma_start(w_peer[:, :, :], w_q_v[:, :, bass.ds(h * 2 * HALF + c * HALF, HALF)])\
                    .then_inc(wq_in[c], 16)
                if c == 0:
                    sp.wait_ge(keys_used, h)
                    sp.dma_start(keys[:, :, :], subkeys_v[:, bass.ds(h * 2, 2), :]).then_inc(keys_in, 16)

            def sweep(i, choosing):
                for b in range(TOPK):
                    if choosing and b in WQ_LOADS:
                        load_wq(i + 2, WQ_LOADS.index(b))
                    sp.wait_ge(uT_half1_ps[b % 2], TOPK // 2 * i + b // 2)
                    sp.dma_start(u_tile[b % 2][:, :], u_table[bass.ds(i * TOPK * P + b * P, P), :])\
                        .then_inc(u_tile_in[b % 2], 16)

            sp.dma_start(w_peer[:, :, :], w_q_v[:, :, HALF:2 * HALF]).then_inc(wq_in[1], 16)
            sp.wait_ge(wq_ready, 1)
            sp.dma_start(w_peer0[:, :, :], w_q_v[:, :, 2 * HALF:3 * HALF]).then_inc(wq_in[0], 16)
            sp.wait_ge(keys_used, 1)
            sp.dma_start(keys[:, :, :], subkeys_v[:, 2:4, :]).then_inc(keys_in, 16)
            sp.wait_ge(wq_ready, 2)
            sp.dma_start(w_peer[:, :, :], w_q_v[:, :, 3 * HALF:4 * HALF]).then_inc(wq_in[1], 16)
            sp.wait_ge(wq_ready, 3)
            with sp.Fori(0, PEER_HEADS - 2) as i:
                sweep(i, choosing=True)
            sp.wait_ge(wq_used, 2 * PEER_HEADS)
            sp.dma_start(x_rows[:, 1:TB, :], x_mid.rearrange("t p d -> p t d")).then_inc(x_back, 16)
            with sp.Fori(PEER_HEADS - 2, PEER_HEADS) as i:
                sweep(i, choosing=False)
            sp.wait_ge(v0_used[1], TILES // 2)
            sp.dma_start(out_v[0], x_rows[:, 0, :]).then_inc(out_stored, 16)
            for t in range(1, TB):
                sp.wait_ge(rows_added, (PEER_HEADS - 1) * SWEPT_BLOCKS + t)
                sp.dma_start(out_v[t], x_rows[:, t, :]).then_inc(out_stored, 16)
            sp.wait_ge(out_stored, 16 * TB)

        @nc_block.gpsimd
        def _(pool):
            pool.memset(ident[:, :], 0.0).then_inc(const_step, 1)
            pool.iota(iota16[:, :], [[1, TOPK]], base=0, channel_multiplier=0,
                      allow_small_or_imprecise_dtypes=True).then_inc(const_step, 1)
            pool.iota(alibi[:, :], [[1, SEQ]], base=-(SEQ - P), channel_multiplier=-1,
                      allow_small_or_imprecise_dtypes=True).then_inc(const_step, 1)
            pool.iota(token_col[:, :], [[P, SWEPT_BLOCKS]], base=0, channel_multiplier=1,
                      allow_small_or_imprecise_dtypes=True).then_inc(const_step, 1)
            pool.memset(minus_half[:, :], -0.5).then_inc(const_step, 1)
            pool.wait_ge(const_step, 5)
            pool.affine_select(out=ident[:, :], in_=ident[:, :], compare_op=ALU.not_equal, fill=1.0,
                               base=0, pattern=[[-1, P]], channel_multiplier=1).then_inc(const_step, 1)
            pool.affine_select(out=alibi[:, :], in_=alibi[:, :], compare_op=ALU.is_ge, fill=MASKED,
                               base=SEQ - P, pattern=[[-1, SEQ]], channel_multiplier=1).then_inc(const_step, 1)
            for i, row in ((0, q_norm_g), (1, k_norm_g)):
                for c in range(2):
                    pool.dma_start(vec_rows[i:i + 1, c * HD:(c + 1) * HD], row[0:1, :]).then_inc(vec_in, 16)
            pool.dma_start(vec_rows[V_SUB:V_SUB + 1, :], subln_g[0:1, :]).then_inc(vec_in, 16)
            pool.dma_start(vec_rows[V_CONV:N_VEC, :], conv_w[0].rearrange("j (c p) -> (j c) p", p=P))\
                .then_inc(vec_in, 16)
            for i, row in enumerate((lambda_q1, lambda_k1, lambda_q2, lambda_k2)):
                pool.dma_start(lam_in[:, i, :], row[0:1, :].to_broadcast([P, HD])).then_inc(vec_in, 16)

            def inverse_root(a):
                return nc.gpsimd.tensor_tensor(a, a, minus_half[:, 0:a.shape[1]], ALU.pow)

            def norm(n):
                for i in range(n * TB, (n + 1) * TB):
                    pool.wait_ge(mean_ready, i + 1)
                    inverse_root(rstd[:, i:i + 1]).then_inc(rstd_ready, 1)

            norm(0)
            with pool.Fori(0, HEADS) as j:
                pool.wait_ge(qk_mean, j + 1)
                inverse_root(qk_ss[:, :]).then_inc(qk_rstd, 1)
                pool.wait_ge(o_mean, j + 1)
                inverse_root(o_ss[:, :]).then_inc(o_rstd, 1)
                pool.wait_ge(o_out, j + 1)
                pool.dma_start(mix_all[bass.ds(j, 1)].rearrange("k p t -> (k p) t"), o_mix).then_inc(o_stored, 16)
                pool.wait_ge(conv_out, j + 1)
                pool.dma_start(mix_all[bass.ds(j + HEADS, 1)].rearrange("k p t -> (k p) t"), b_sb)\
                    .then_inc(conv_stored, 16)
            norm(1)

            with pool.Fori(0, PEER_HEADS) as i:
                for b in range(TOPK):
                    which, col = divmod(b, TOPK // 2)
                    if col == 0:
                        pool.wait_ge(chosen, TB * i + 1)
                        nc.gpsimd.tensor_copy(experts0[:, which, :],
                                              experts[:, 0, bass.ds(i * TOPK + b, TOPK // 2)]).then_inc(staged0, 1)
                        pool.wait_ge(staged0, 2 * i + which + 1)
                        pool.sem_inc(pool_past, 1)
                    index = bass.IndirectOffsetOnAxis(ap=experts0[:, which, col:col + 1], axis=0)
                    pool.wait_ge(u_used[b % 2], TOPK // 2 * i + b // 2)
                    pool.sem_inc(pool_past, 1)
                    pool.indirect_dma_start(out=u_row[b % 2][:, :], out_offset=None, in_=u_table,
                                            in_offset=index).then_inc(u_in[b % 2], 16)
                    pool.wait_ge(v0_used[b % 2], TOPK // 2 * i + b // 2)
                    pool.sem_inc(pool_past, 1)
                    pool.indirect_dma_start(out=v_row[b % 2][:, :], out_offset=None, in_=v_table,
                                            in_offset=index).then_inc(v0_in[b % 2], 16)

            def stage(n, h, t):
                cols = slice(h * TOPK, (h + 1) * TOPK) if isinstance(h, int) else bass.ds(h * TOPK, TOPK)
                nc.gpsimd.tensor_copy(experts_at[:, t - 1, :], experts[:, t, cols]).then_inc(staged, 1)
                nc.gpsimd.tensor_copy(cells_at[:, t - 1, :], cells[:, t - 1, cols]).then_inc(staged, 1)
                pool.wait_ge(staged, 2 * n + 2)
                pool.sem_inc(pool_past, 1)

            def fetch_product(t, s):
                pool.indirect_dma_start(
                    out=dots[:, s:s + 1], out_offset=None, in_=products_all,
                    in_offset=bass.IndirectOffsetOnAxis(ap=cells_at[:, t - 1, s:s + 1], axis=0))\
                    .then_inc(cells_in, 16)

            def gather_v(n, t, s):
                pool.wait_ge(v_used[s % RING], TOPK // RING * n + s // RING)
                pool.sem_inc(pool_past, 1)
                pool.indirect_dma_start(
                    out=v_ring[s % RING][:, :], out_offset=None, in_=v_table,
                    in_offset=bass.IndirectOffsetOnAxis(ap=experts_at[:, t - 1, s:s + 1], axis=0))\
                    .then_inc(v_in[s % RING], 16)

            def head(h, last):
                for t in range(1, TB):
                    n = SWEPT_BLOCKS * h + t - 1
                    then = t % SWEPT_BLOCKS + 1
                    ahead = not (last and t == TB - 1)
                    if ahead:
                        pool.wait_ge(gelu_done, n + 1)
                        pool.sem_inc(pool_past, 1)
                    for s in range(RING, TOPK):
                        gather_v(n, t, s)
                        if ahead:
                            fetch_product(then, 2 * (s - RING))
                            fetch_product(then, 2 * (s - RING) + 1)
                    if ahead:
                        for s in range(RING):
                            gather_v(n + 1, then, s)
                    if t == 1:
                        stage(n + 2, h, 3)
                    elif not last:
                        stage(n + 2, h + 1, t - 1)

            pool.wait_ge(cells_ready, 1)
            stage(0, 0, 1)
            stage(1, 0, 2)
            for b in range(2):
                pool.wait_ge(uT_half1_ps[b], TILES // 2)
                gather_v(0, 1, b)
            for b in range(2):
                pool.wait_ge(swept[b], TILES // 2)
            gather_v(0, 1, 2)
            for b in range(2):
                pool.wait_ge(swept_stored[b], 16 * TILES // 2)
            for s in range(TOPK):
                fetch_product(1, s)
                if s % 2 == 1 and 3 + s // 2 < RING:
                    gather_v(0, 1, 3 + s // 2)
            with pool.Fori(0, PEER_HEADS - 1) as h:
                head(h, last=False)
            head(PEER_HEADS - 1, last=True)

        @nc_block.scalar
        def _(act):
            steps = Steps(act, act_step)

            def norm(n):
                for t in range(TB + 1):
                    if t < TB:
                        if n == 0:
                            act.wait_ge(x_in[t], 16)
                        else:
                            act.wait_ge(out_added[t], OUT_CHUNKS)
                        if n * TB + t > 0:
                            act.wait_ge(ssq_ready, n * TB + t)
                        nc.scalar.activation(squares[:, :], x_rows[:, t, :], ACT.Square,
                                             accum_out=ssq[:, n * TB + t:n * TB + t + 1]).then_inc(ssq_ready, 1)
                    if t > 0:
                        act.wait_ge(hT_ps, n * TB + t)
                        for b in range(4):
                            nc.scalar.activation(hT_hi[:, 4 * b:4 * b + 4, (t - 1) * P:t * P],
                                                 ps[:, 4 + b, :].rearrange("p (k t) -> p k t", k=4),
                                                 ACT.Copy).then_inc(hT_hi_ready, 1)

            def split_weights(c, q, before, done):
                n = c + before
                act.wait_ge(w_in_raw[q % 2], 16 * (2 * n + q // 2 + 1))
                act.wait_ge(*((w_used[q - 2], n + 1) if q >= 2 else (w_used[2], n) if q == 0 else (done[TB - 1], c)))
                nc.scalar.activation(w_hi[q % 2][:, :, :], w_raw[q % 2][:, :, :], ACT.Copy).then_inc(w_hi_ready, 1)

            norm(0)

            def split_wi(c, q):
                split_weights(c, q, 0, proj_done)

            def keep_qkv(c):
                for t in (0, 2):
                    act.wait_ge(proj_done[t], c + 1)
                    nc.scalar.activation(qkv[:, t, bass.ds(c * CHUNK, CHUNK)], ps[:, t, :], ACT.Copy)\
                        .then_inc(proj_kept[t], 1)

            def split_wc(j, p):
                act.wait_ge(wc_in[p % 2], 16 * (PIECES // 2 * j + p // 2 + 1))
                before_j, before = (j, p - PIECE_RING) if p >= PIECE_RING else (j - 1, p + PIECE_RING)
                if not (isinstance(before_j, int) and before_j < 0):
                    act.wait_ge(*((wc_half_used, PIECES // 2 * before_j + before // 2 + 1) if before % 2 == 0
                                  else (conv_done[before // 2], before_j + 1)))
                nc.scalar.activation(wc_hi[:, p % PIECE_RING, :, :], wc_raw[p % 2][:, :, :], ACT.Copy)\
                    .then_inc(wc_hi_ready, 1)

            chunks = QKV_CHUNKS
            split_wi(0, 0)
            split_wi(0, 1)
            act.wait_ge(lam_sum, 1)
            nc.scalar.activation(lam[:, 2:4], lam[:, 0:2], ACT.Exp).then_inc(lam_exp, 1)
            with act.Fori(0, chunks - 1) as c:
                split_wi(c, 2)
                split_wi(c, 3)
                split_wi(c + 1, 0)
                keep_qkv(c)
                split_wi(c + 1, 1)
            split_wi(chunks - 1, 2)
            split_wi(chunks - 1, 3)
            for p in range(PIECE_RING):
                split_wc(0, p)
            keep_qkv(chunks - 1)
            act.wait_ge(vec_ready, 1)

            def head(j, last):
                def exps(qb):
                    act.wait_ge(max_ready, TB * j + qb + 1)
                    for c in range(2):
                        part = probs[:, qb % 2, c, 0:(qb + 1) * P]
                        nc.scalar.activation(part, part, ACT.Exp, bias=neg_max[:, qb % 2, c:c + 1],
                                             accum_out=row_sum[:, qb % 2, c:c + 1]).then_inc(exp_done, 1)

                def keep_aT(qb):
                    act.wait_ge(a_turned[qb % 2], 2 * j + qb // 2 + 1)
                    act.wait_ge(av_done[qb % 2], 2 * j + qb // 2)
                    nc.scalar.activation(aT[:, qb % 2, 0:(qb + 1) * P], ps[:, 6, 0:(qb + 1) * P], ACT.Copy)\
                        .then_inc(aT_ready, 1)

                split_wc(j, 3)
                act.wait_ge(conv_done[0], j + 1)
                act.wait_ge(conv_stored, 16 * j)
                nc.scalar.activation(b_sb, ps[:, 0, :], ACT.Copy).then_inc(b_kept, 1)
                split_wc(j, 4)
                for i in range(2):
                    act.wait_ge(qkT_ps, 2 * j + i + 1)
                    nc.scalar.activation(qkT[:, i, :], ps[:, 6 + i, :], ACT.Copy,
                                         scale=vec[:, V_Q + i:V_Q + i + 1]).then_inc(qkT_ready, 1)
                exps(0)
                exps(1)
                keep_aT(0)
                split_wc(j, 5)
                exps(2)
                act.wait_ge(conv_done[1], j + 1)
                act.wait_ge(conv_gated, j)
                nc.scalar.activation(c_sb, ps[:, 1, :], ACT.Copy).then_inc(c_kept, 1)
                if not last:
                    split_wc(j + 1, 0)
                keep_aT(1)
                exps(3)
                keep_aT(2)
                if not last:
                    split_wc(j + 1, 1)
                keep_aT(3)
                act.wait_ge(av_done[1], 2 * j + 2)
                act.wait_ge(o_stored, 16 * j)
                nc.scalar.activation(o_sq, ps[:, 7, :], ACT.Square).then_inc(o_squared, 1)
                if not last:
                    split_wc(j + 1, 2)
                act.wait_ge(oT_ps, j + 1)
                nc.scalar.activation(o_mix, ps[:, 6, :], ACT.Copy, scale=vec[:, V_SUB:V_SUB + 1]).then_inc(o_out, 1)

            with act.Fori(0, HEADS - 1) as j:
                head(j, last=False)
            head(HEADS - 1, last=True)

            def split_wo(c, q):
                split_weights(c, q, QKV_CHUNKS, out_done)

            def split_mix(q):
                act.wait_ge(mix_in[q], 16)
                nc.scalar.activation(mix_hi[:, QUARTER * q:QUARTER * (q + 1), :],
                                     mixT[:, QUARTER * q:QUARTER * (q + 1), :], ACT.Copy).then_inc(mix_hi_ready, 1)

            chunks = OUT_CHUNKS
            act.wait_ge(conv_done[2], CT)
            split_mix(0)
            act.wait_ge(conv_out, CT)
            split_wo(0, 0)
            split_mix(2)
            split_wo(0, 1)
            split_mix(1)
            split_mix(3)
            for t in range(TB):
                act.dma_start(x_rows[:, t, :], x_v[t]).then_inc(x_in[t], 16)
            act.dma_start(gain, ffn_norm_g[0:1, :].to_broadcast([P, D])).then_inc(gain_in, 16)
            with act.Fori(0, chunks - 1) as c:
                split_wo(c, 2)
                split_wo(c, 3)
                split_wo(c + 1, 0)
                split_wo(c + 1, 1)
            split_wo(chunks - 1, 2)
            split_wo(chunks - 1, 3)
            norm(1)

            def split_wq(h, c, early=False):
                act.wait_ge(wq_in[c], 16 * h + 16)
                before = 2 * h + c - 1 if early else 2 * h + c
                second = c == 1 or not early
                raw, high = (w_peer, wq_hi) if second else (w_peer0, wq0_hi)
                if before > 0:
                    act.wait_ge(wq_used, before)
                nc.scalar.activation(high[:, :, :], raw[:, :, :], ACT.Copy).then_inc(wq_hi_ready, 1)

            def queries_out(h, c):
                act.wait_ge(wq_used, 2 * h + c + 1)
                nc.scalar.activation(pqT[:, c, :], ps_pq, ACT.Copy).then_inc(pqT_ready, 1)
                if c == 0:
                    act.wait_ge(keys_used, h + 1)
                    nc.scalar.activation(keysT[:, :, :], ps_keysT, ACT.Copy).then_inc(keysT_ready, 1)

            def key_scores_out(h):
                act.wait_ge(key_scores_read, TB * h)
                for c in range(2):
                    act.wait_ge(key_scores_ps, 2 * h + c + 1)
                    nc.scalar.activation(key_scores[:, c, :, :], ps_key_scores[c], ACT.Copy)\
                        .then_inc(key_scores_ready, 1)

            def exp_gates(h, t):
                act.wait_ge(top_ready, TB * h + t + 1)
                nc.scalar.activation(gate_exps[:, t, :], top[:, t, :], ACT.Exp, bias=neg_top[:, t:t + 1],
                                     accum_out=gate_sum[:, t:t + 1]).then_inc(gates_exp, 1)

            act.wait_ge(h_ready, 2 * TB)
            split_wq(0, 0, early=True)
            split_wq(0, 1, early=True)
            queries_out(0, 0)
            split_wq(1, 0, early=True)
            queries_out(0, 1)
            split_wq(1, 1, early=True)
            key_scores_out(0)
            exp_gates(0, 0)
            queries_out(1, 0)
            exp_gates(0, 1)
            queries_out(1, 1)

            def split_u(i, b, half):
                if half == 0:
                    act.wait_ge(uT_half0_ps, TOPK * i + b + 1)
                else:
                    act.wait_ge(uT_half1_ps[b % 2], TOPK // 2 * i + b // 2 + 1)
                nc.scalar.activation(uT_hi[half][:, :, :], ps_uT[half], ACT.Copy).then_inc(uT_hi_ready[half], 1)

            def sweep(i, querying, choosing, last=False):
                for b in range(TOPK):
                    more = not (last and b == TOPK - 1)
                    act.wait_ge(u_used[b % 2], TOPK // 2 * i + b // 2 + 1)
                    nc.scalar.activation(gelus0[:, b:b + 1], dots0[:, b:b + 1], ACT.Gelu).then_inc(gelu0_done, 1)
                    if more:
                        split_u(i, b + 1, 0)
                    act.wait_ge(swept[b % 2], TOPK // 2 * i + b // 2 + 1)
                    act.wait_ge(swept_stored[b % 2], 16 * (TOPK // 2 * i + b // 2))
                    nc.scalar.activation(products[b % 2][:, :], ps[:, 4 + b % 2, 0:SWEPT], ACT.Copy)\
                        .then_inc(swept_kept[b % 2], 1)
                    act.wait_ge(swept_kept[b % 2], TOPK // 2 * i + b // 2 + 1)
                    act.dma_start(products_v[bass.ds(i * TOPK * P + b * P, P), :], products[b % 2][:, :])\
                        .then_inc(swept_stored[b % 2], 16)
                    if more:
                        split_u(i, b + 1, 1)
                    if querying and b in SPLIT_WQ:
                        split_wq(i + 2, SPLIT_WQ.index(b))
                    if querying and b in QUERIES_OUT:
                        queries_out(i + 2, QUERIES_OUT.index(b))
                    if choosing and b % 4 == 3:
                        exp_gates(i + 1, b // 4)
                if querying:
                    key_scores_out(i + 2)

            split_u(0, 0, 0)
            split_u(0, 0, 1)
            exp_gates(0, 2)
            exp_gates(0, 3)
            key_scores_out(1)
            with act.Fori(0, PEER_HEADS - 2) as i:
                sweep(i, querying=True, choosing=True)
            sweep(PEER_HEADS - 2, querying=False, choosing=True)
            sweep(PEER_HEADS - 1, querying=False, choosing=False, last=True)

            def gelu(n):
                act.wait_ge(cells_in, 16 * TOPK * (n + 1))
                act.wait_ge(acts_ready, n)
                nc.scalar.activation(gelus[:, :], dots[:, :], ACT.Gelu).then_inc(gelu_done, 1)

            with act.Fori(0, PEER_HEADS * SWEPT_BLOCKS) as n:
                gelu(n)

        @nc_block.vector
        def _(dve):
            v = nc.vector
            steps = Steps(dve, dve_step)
            link, done = steps.link, steps.done

            def past():
                dve.sem_inc(dve_past, 1)

            def norm(n):
                for t in range(TB + 1):
                    i = n * TB + t
                    if t < TB:
                        dve.wait_ge(ssq_ready, i + 1)
                        v.tensor_scalar(rstd[:, i:i + 1], ssq[:, i:i + 1], 1.0 / D, EPS, ALU.mult, ALU.add)\
                            .then_inc(mean_ready, 1)
                        dve.wait_ge(rstd_ready, i + 1)
                        if t == 0:
                            dve.wait_ge(gain_in, 16 * (n + 1))
                        v.scalar_tensor_tensor(out=h_rows[:, t, :], in0=x_rows[:, t, :], scalar=rstd[:, i:i + 1],
                                               in1=gain, op0=ALU.mult, op1=ALU.mult).then_inc(h_ready, 1)
                    if t > 0:
                        dve.wait_ge(hT_ps, i)
                        for b in range(4):
                            bank = ps[:, 4 + b, :].rearrange("p (k t) -> p k t", k=4)
                            part = slice(4 * b, 4 * b + 4), slice((t - 1) * P, t * P)
                            low = hT_lo if n == 0 else h2T_lo
                            dve.wait_ge(hT_hi_ready, 4 * (i - 1) + b + 1)
                            v.tensor_tensor(low[:, *part], bank, hT_hi[:, *part].bitcast(F32), ALU.subtract)\
                                .then_inc(hT_ready, 1)

            def split_weights(c, q, before, w_lo):
                dve.wait_ge(w_hi_ready, 4 * (c + before) + q + 1)
                v.tensor_tensor(w_lo[q % 2][:, :, :], w_raw[q % 2][:, :, :], w_hi[q % 2][:, :, :].bitcast(F32),
                                ALU.subtract).then_inc(w_ready, 1)

            norm(0)

            def split_wi(c, q):
                split_weights(c, q, 0, wi_lo)

            def keep_qkv(c):
                for t in (1, 3):
                    dve.wait_ge(proj_done[t], c + 1)
                    v.tensor_copy(qkv[:, t, bass.ds(c * CHUNK, CHUNK)], ps[:, t, :]).then_inc(proj_kept[t], 1)

            def split_wc(j, p):
                dve.wait_ge(wc_hi_ready, PIECES * j + p + 1)
                v.tensor_tensor(wc_lo[:, p % PIECE_RING, :, :], wc_raw[p % 2][:, :, :],
                                wc_hi[:, p % PIECE_RING, :, :].bitcast(F32), ALU.subtract).then_inc(wc_ready, 1)

            chunks = QKV_CHUNKS
            split_wi(0, 0)
            split_wi(0, 1)

            dve.wait_ge(vec_in, 16 * 10)
            for i in range(2):
                link(v.tensor_tensor(lam_prod[:, :], lam_in[:, 2 * i, :], lam_in[:, 2 * i + 1, :], ALU.mult))
                ins = v.reduce_sum(lam[:, i:i + 1], lam_prod[:, :], axis=AX.X)
                if i == 0:
                    link(ins)
                else:
                    ins.then_inc(lam_sum, 1)
            dve.wait_ge(vec_ps, 1)
            link(v.tensor_copy(vec[:, :], ps[:, 4, 0:N_VEC]))
            link(v.tensor_scalar(vec[:, V_Q:V_Q + 1], vec[:, V_Q:V_Q + 1], HD ** -0.5, None, ALU.mult))
            v.tensor_scalar(vec[:, V_SUB:V_SUB + 1], vec[:, V_SUB:V_SUB + 1], 1.0 - LAM_INIT, None, ALU.mult)\
                .then_inc(vec_ready, 1)
            dve.wait_ge(lam_exp, 1)
            link(v.tensor_tensor(neg_lam[:, :], lam[:, 3:4], lam[:, 2:3], ALU.subtract))
            link(v.tensor_scalar(neg_lam[:, :], neg_lam[:, :], -LAM_INIT, None, ALU.add))

            with dve.Fori(0, chunks - 1) as c:
                split_wi(c, 2)
                split_wi(c, 3)
                split_wi(c + 1, 0)
                keep_qkv(c)
                split_wi(c + 1, 1)
            split_wi(chunks - 1, 2)
            split_wi(chunks - 1, 3)
            dve.wait_ge(w_used[2], chunks)
            split_wc(0, 0)
            split_wc(0, 1)
            keep_qkv(chunks - 1)
            split_wc(0, 2)
            for t in range(TB):
                dve.wait_ge(proj_kept[t], chunks)

            def head(j, last):
                dve.wait_ge(qkT_ps, 2 * j)
                rows = [qkv[:, :, bass.ds(i * ATTN + j * P, P)] for i in range(2)]
                done(v.tensor_tensor(sq[:, 0, :].rearrange("p (t n) -> p t n", t=TB), rows[0], rows[0], ALU.mult))
                link(v.tensor_tensor(sq[:, 1, :].rearrange("p (t n) -> p t n", t=TB), rows[1], rows[1], ALU.mult))
                link(v.reduce_sum(qk_ss[:, :], sq[:, :, :].rearrange("p a (g d) -> p (a g) d", d=HD), axis=AX.X))
                v.tensor_scalar(qk_ss[:, :], qk_ss[:, :], 1.0 / HD, EPS, ALU.mult, ALU.add).then_inc(qk_mean, 1)
                dve.wait_ge(qk_rstd, j + 1)
                for i in range(2):
                    v.tensor_tensor(qk_n[:, i, :].rearrange("p (t c d) -> p t c d", t=TB, c=2),
                                    rows[i].rearrange("p t (c d) -> p t c d", c=2),
                                    qk_ss[:, 8 * i:8 * i + 8].rearrange("p (t c) -> p t c", c=2).unsqueeze(3)
                                    .to_broadcast([P, TB, 2, HD]), ALU.mult).then_inc(qk_normed, 1)
                split_wc(j, 3)
                split_wc(j, 4)
                done(v.tensor_scalar(alibi[:, :], alibi[:, :], 0.5, None, ALU.mult))
                link(v.tensor_copy(conv_taps[:, :, :],
                                   vec[:, V_CONV:N_VEC].rearrange("p (a c) -> p a c", a=TAPS)[:, :, bass.ds(j, 1)]))

                def biased(qb):
                    n = (qb + 1) * P
                    dve.wait_ge(scores_done, TB * j + qb + 1)
                    dve.wait_ge(a_turned[qb % 2], 2 * j + qb // 2)
                    past()
                    for c in range(2):
                        v.tensor_tensor_reduce(out=probs[:, qb % 2, c, 0:n], in0=ps[:, 2 + 2 * (qb % 2) + c, 0:n],
                                               in1=alibi[:, SEQ - n:SEQ], scale=1.0, scalar=LOWEST,
                                               op0=ALU.add, op1=ALU.max, accum_out=row_max[:, qb % 2, c:c + 1])\
                            .then_inc(scores_read[qb % 2], 1)
                    dve.wait_ge(scores_read[qb % 2], 4 * j + 2 * (qb // 2) + 2)
                    v.tensor_scalar(neg_max[:, qb % 2, :], row_max[:, qb % 2, :], -1.0, None, ALU.mult)\
                        .then_inc(max_ready, 1)

                def combined(qb):
                    n, i = (qb + 1) * P, qb % 2
                    dve.wait_ge(exp_done, 2 * (TB * j + qb) + 2)
                    link(v.reciprocal(inv_sum[:, i, :], row_sum[:, i, :]))
                    link(v.tensor_tensor(inv_sum[:, i, 1:2], inv_sum[:, i, 1:2], neg_lam[:, :], ALU.mult))
                    link(v.tensor_scalar(probs[:, i, 1, 0:n], probs[:, i, 1, 0:n], inv_sum[:, i, 1:2], None, ALU.mult))
                    past()
                    v.scalar_tensor_tensor(out=probs[:, i, 0, 0:n], in0=probs[:, i, 0, 0:n],
                                           scalar=inv_sum[:, i, 0:1], in1=probs[:, i, 1, 0:n],
                                           op0=ALU.mult, op1=ALU.add).then_inc(a_ready, 1)

                biased(0)
                biased(1)
                combined(0)
                biased(2)
                split_wc(j, 5)
                combined(1)
                biased(3)
                if not last:
                    split_wc(j + 1, 0)
                combined(2)
                combined(3)
                if not last:
                    split_wc(j + 1, 1)
                dve.wait_ge(o_squared, j + 1)
                link(v.reduce_sum(o_ss[:, :], o_sq.rearrange("p (t n) -> p t n", t=TB), axis=AX.X))
                v.tensor_scalar(o_ss[:, :], o_ss[:, :], 1.0 / VD, EPS, ALU.mult, ALU.add).then_inc(o_mean, 1)
                dve.wait_ge(o_rstd, j + 1)
                dve.wait_ge(oT_ps, j)
                v.tensor_tensor(o_n.rearrange("p (t n) -> p t n", t=TB),
                                ps[:, 7, :].rearrange("p (t n) -> p t n", t=TB),
                                o_ss[:, :].unsqueeze(2).to_broadcast([P, TB, VD]), ALU.mult).then_inc(o_normed, 1)
                if not last:
                    split_wc(j + 1, 2)
                dve.wait_ge(c_kept, j + 1)
                dve.wait_ge(conv_done[2], j + 1)
                v.tensor_tensor(conv_u, ps[:, 0, :], c_sb, ALU.mult).then_inc(conv_gated, 1)
                dve.wait_ge(conv_gated, j + 1)
                link(v.tensor_scalar(conv_y, conv_u, conv_taps[:, 2, :], None, ALU.mult))
                for lag in (1, 2):
                    past()
                    link(v.scalar_tensor_tensor(out=conv_y[:, lag:], in0=conv_u[:, 0:SEQ - lag],
                                                scalar=conv_taps[:, 2 - lag, :], in1=conv_y[:, lag:],
                                                op0=ALU.mult, op1=ALU.add))
                dve.wait_ge(b_kept, j + 1)
                v.tensor_tensor(b_sb, conv_y, b_sb, ALU.mult).then_inc(conv_out, 1)
                dve.wait_ge(conv_out, j + 1)

            with dve.Fori(0, HEADS - 1) as j:
                steps.enter(j, 21)
                head(j, last=False)
                steps.leave(HEADS - 1)
            head(HEADS - 1, last=True)

            def split_wo(c, q):
                split_weights(c, q, QKV_CHUNKS, wo_lo)

            def split_mix(q):
                dve.wait_ge(mix_hi_ready, MIX_ORDER.index(q) + 1)
                part = slice(QUARTER * q, QUARTER * (q + 1))
                v.tensor_tensor(mix_lo[:, part, :], mixT[:, part, :], mix_hi[:, part, :].bitcast(F32), ALU.subtract)\
                    .then_inc(mix_ready, 1)

            def add_mixed(c):
                for t in range(TB):
                    part = x_rows[:, t, bass.ds(c * CHUNK, CHUNK)]
                    dve.wait_ge(out_done[t], c + 1)
                    v.tensor_tensor(part, ps[:, t, :], part, ALU.add).then_inc(out_added[t], 1)

            chunks = OUT_CHUNKS
            split_mix(0)
            split_wo(0, 0)
            split_mix(2)
            split_wo(0, 1)
            split_mix(1)
            split_mix(3)
            for t in range(TB):
                dve.wait_ge(x_in[t], 32)
            with dve.Fori(0, chunks - 1) as c:
                split_wo(c, 2)
                split_wo(c, 3)
                split_wo(c + 1, 0)
                add_mixed(c)
                split_wo(c + 1, 1)
            split_wo(chunks - 1, 2)
            split_wo(chunks - 1, 3)
            add_mixed(chunks - 1)
            norm(1)

            def top16(values, indices, source, remains):
                past()
                link(v.max(values[:, 0:8], source))
                past()
                done(v.max_index(indices[:, 0:8], values[:, 0:8], source))
                link(v.match_replace(remains, values[:, 0:8], source, LOWEST))
                past()
                link(v.max(values[:, 8:16], remains))
                past()
                link(v.max_index(indices[:, 8:16], values[:, 8:16], remains))

            def choose_half(t, c):
                top16(half_top[:, c, :], half_idx[:, c, :], key_scores[:, c, t, :], rest[:, :])

            def choose_pairs(unit, t):
                v.tensor_scalar(half_num[:, 0, :], half_idx[:, 0, :], float(N_KEYS), None, ALU.mult)\
                    .then_inc(key_scores_read, 1)
                done(v.tensor_copy(half_num[:, 1, :], half_idx[:, 1, :]))
                link(v.tensor_tensor(cand[:, :, :],
                                     half_top[:, 0, :].unsqueeze(2).to_broadcast([P, TOPK, TOPK]),
                                     half_top[:, 1, :].unsqueeze(1).to_broadcast([P, TOPK, TOPK]), ALU.add))
                top16(top[:, t, :], top_idx, cand[:, :, :].rearrange("p a b -> p (a b)"), cand_rest[:, :])
                v.tensor_scalar(neg_top[:, t:t + 1], top[:, t, 0:1], -1.0, None, ALU.mult).then_inc(top_ready, 1)

            def choose_experts(unit, t, cols):
                done(v.tensor_scalar(pair[:, 0, :], top_idx[:, :], 4, None, ALU.logical_shift_right))
                link(v.tensor_scalar(pair[:, 1, :], top_idx[:, :], TOPK - 1, None, ALU.bitwise_and))
                link(v.tensor_copy(pair_num[:, :, :], pair[:, :, :]))
                link(v.tensor_tensor(pick[:, :, :, :].rearrange("p c s a -> p (c s) a"),
                                     pair_num[:, :, :].rearrange("p c s -> p (c s)").unsqueeze(2)
                                     .to_broadcast([P, 2 * TOPK, TOPK]),
                                     iota16[:, :].unsqueeze(1).to_broadcast([P, 2 * TOPK, TOPK]), ALU.is_equal))
                dve.wait_ge(key_scores_read, unit + 1)
                link(v.tensor_tensor(pick[:, :, :, :], pick[:, :, :, :],
                                     half_num[:, :, :].unsqueeze(2).to_broadcast([P, 2, TOPK, TOPK]), ALU.mult))
                link(v.reduce_sum(picked[:, :, :].rearrange("p c s -> p (c s)"),
                                  pick[:, :, :, :].rearrange("p c s a -> p (c s) a"), axis=AX.X))
                v.tensor_tensor(experts[:, t, cols], picked[:, 0, :], picked[:, 1, :], ALU.add)\
                    .then_inc(chosen, 1)

            def choose(h, slot):
                t = slot // 4
                if slot == 0:
                    dve.wait_ge(key_scores_ready, 2 * h + 2)
                if slot % 4 < 2:
                    choose_half(t, slot % 4)
                elif slot % 4 == 2:
                    choose_pairs(TB * h + t, t)
                else:
                    choose_experts(TB * h + t, t, bass.ds(h * TOPK, TOPK))

            def choose_gates(h):
                dve.wait_ge(gates_exp, TB * h + TB)
                link(v.reciprocal(gate_inv[:, :], gate_sum[:, :]))
                link(v.tensor_tensor(gates[:, :, bass.ds(h * TOPK, TOPK)], gate_exps[:, :, :],
                                     gate_inv[:, :].unsqueeze(2).to_broadcast([P, TB, TOPK]), ALU.mult))

            def split_wq(h, c, early=False):
                dve.wait_ge(wq_hi_ready, 2 * h + c + 1)
                raw, high, low = (w_peer0, wq0_hi, wq0_lo) if early and c == 0 else (w_peer, wq_hi, wq_lo)
                v.tensor_tensor(low[:, :, :], raw[:, :, :], high[:, :, :].bitcast(F32), ALU.subtract)\
                    .then_inc(wq_ready, 1)

            for g in range(4):
                split_wq(g // 2, g % 2, early=True)
            for slot in range(3 * TOPK // 4):
                choose(0, slot)

            def split_u(c, half):
                dve.wait_ge(uT_hi_ready[half], c + 1)
                v.tensor_tensor(uT_lo[half][:, :, :], ps_uT[half], uT_hi[half][:, :, :].bitcast(F32), ALU.subtract)\
                    .then_inc(uT_ready[half], 1)

            def sweep(i, querying, choosing, last=False):
                for b in range(TOPK):
                    c = TOPK * i + b
                    use = TOPK // 2 * i + b // 2 + 1
                    dve.wait_ge(u_in[b % 2], 16 * use)
                    v.tensor_tensor_reduce(out=u_row[b % 2][:, :], in0=u_row[b % 2][:, :], in1=h_rows[:, 0, :],
                                           scale=1.0, scalar=0.0, op0=ALU.mult, op1=ALU.add,
                                           accum_out=dots0[:, b:b + 1]).then_inc(u_used[b % 2], 1)
                    if not (last and b == TOPK - 1):
                        split_u(c + 1, 0)
                    dve.wait_ge(gelu0_done, c + 1)
                    link(v.tensor_tensor(acts0[:, b:b + 1], gelus0[:, b:b + 1],
                                         gates[:, 0, bass.ds(i * TOPK + b, 1)], ALU.mult))
                    dve.wait_ge(v0_in[b % 2], 16 * use)
                    past()
                    v.scalar_tensor_tensor(out=x_rows[:, 0, :], in0=v_row[b % 2][:, :], scalar=acts0[:, b:b + 1],
                                           in1=x_rows[:, 0, :], op0=ALU.mult, op1=ALU.add)\
                        .then_inc(v0_used[b % 2], 1)
                    if not (last and b == TOPK - 1):
                        split_u(c + 1, 1)
                    dve.wait_ge(v0_used[b % 2], use)
                    if querying and b in SPLIT_WQ:
                        split_wq(i + 2, SPLIT_WQ.index(b))
                    if choosing:
                        choose(i + 1, b)
                    if last and b == 0:
                        dve.wait_ge(chosen, TB * PEER_HEADS)
                        for t in range(1, TB):
                            ins = v.tensor_scalar(cells[:, t - 1, :], experts[:, t, :], float(SWEPT),
                                                  token_col[:, t - 1:t], ALU.mult, ALU.add)
                            if t < TB - 1:
                                done(ins)
                            else:
                                ins.then_inc(cells_ready, 1)
                if choosing:
                    choose_gates(i + 1)

            split_u(0, 0)
            split_u(0, 1)
            for slot in range(3 * TOPK // 4, TOPK):
                choose(0, slot)
            choose_gates(0)
            with dve.Fori(0, PEER_HEADS - 2) as i:
                steps.enter(i, 110)
                sweep(i, querying=True, choosing=True)
                steps.leave(PEER_HEADS - 2)
            sweep(PEER_HEADS - 2, querying=False, choosing=True)
            sweep(PEER_HEADS - 1, querying=False, choosing=False, last=True)
            dve.wait_ge(x_back, 16)

            def weigh(n, h, t):
                cols = slice(h * TOPK, (h + 1) * TOPK) if isinstance(h, int) else bass.ds(h * TOPK, TOPK)
                dve.wait_ge(gelu_done, n + 1)
                v.tensor_tensor(acts[:, :], gelus[:, :], gates[:, t, cols], ALU.mult).then_inc(acts_ready, 1)
                dve.wait_ge(acts_ready, n + 1)

            def spread():
                v.tensor_tensor(diag[:, :, :, :],
                                ident[:, :].unsqueeze(1).unsqueeze(1).to_broadcast([P, 4, 3, P]),
                                acts[:, :].rearrange("p (a b) -> p a b", b=4)[:, :, 0:3].unsqueeze(3)
                                .to_broadcast([P, 4, 3, P]), ALU.mult).then_inc(diag_ready, 1)

            def head(h, last):
                for t in range(1, TB):
                    n = SWEPT_BLOCKS * h + t - 1
                    for s in range(3, TOPK, 4):
                        use = TOPK // RING * n + s // RING + 1
                        dve.wait_ge(v_in[s % RING], 16 * use)
                        past()
                        v.scalar_tensor_tensor(out=x_rows[:, t, :], in0=v_ring[s % RING][:, :],
                                               scalar=acts[:, s:s + 1], in1=x_rows[:, t, :],
                                               op0=ALU.mult, op1=ALU.add).then_inc(v_used[s % RING], 1)
                        dve.wait_ge(v_used[s % RING], use)
                    if not (last and t == TB - 1):
                        weigh(n + 1, h if t < TB - 1 else h + 1, t % SWEPT_BLOCKS + 1)
                    dve.wait_ge(v_used[(TOPK - 2) % RING], TOPK // RING * (n + 1))
                    v.tensor_tensor(x_rows[:, t, :], ps_rows, x_rows[:, t, :], ALU.add).then_inc(rows_added, 1)
                    if not (last and t == TB - 1):
                        spread()

            weigh(0, 0, 1)
            spread()
            with dve.Fori(0, PEER_HEADS - 1) as h:
                head(h, last=False)
            head(PEER_HEADS - 1, last=True)

        @nc_block.tensor
        def _(pe):
            mm, turn = nc.tensor.matmul, nc.tensor.transpose

            def norm(n):
                for t in range(TB):
                    pe.wait_ge(h_ready, n * TB + t + 1)
                    if t > 0:
                        pe.wait_ge(hT_ready, 4 * (n * TB + t))
                    for k in range(KT):
                        last = turn(ps[:, 4 + k // 4, (k % 4) * P:(k % 4 + 1) * P],
                                    h_rows[:, t, k * P:(k + 1) * P], ident[:, :])
                    last.then_inc(hT_ps, 1)

            def split_products(out, a_hi, a_lo, b_hi, b_lo, first, last):
                mm(out, a_hi, b_hi, start=first, stop=False)
                mm(out, a_lo, b_hi, start=False, stop=False)
                return mm(out, a_hi, b_lo, start=False, stop=last)

            def project(chunks, before, w_lo, source_hi, source_lo, finished, kept, order=range(4)):
                with pe.Fori(0, chunks) as c:
                    for q in range(4):
                        pe.wait_ge(w_ready, 4 * (c + before) + q + 1)
                        if finished is out_done:
                            pe.wait_ge(mix_ready, q + 1)
                        for t in range(TB):
                            if q == 0:
                                pe.wait_ge(kept[t], c)
                            tokens = slice(t * P, (t + 1) * P)
                            for k in range(QUARTER):
                                last = split_products(
                                    ps[:, t, :], source_hi[:, QUARTER * order[q] + k, tokens],
                                    source_lo[:, QUARTER * order[q] + k, tokens], w_hi[q % 2][:, k, :], w_lo[q % 2][:, k, :],
                                    q == 0 and k == 0, q == 3 and k == QUARTER - 1)
                            if q == 3:
                                last.then_inc(finished[t], 1)
                        if q < 3:
                            last.then_inc(w_used[q], 1)

            pe.wait_ge(const_step, 7)
            norm(0)
            pe.wait_ge(hT_ready, 4 * TB)
            pe.wait_ge(vec_in, 16 * 10)
            turn(ps[:, 4, 0:N_VEC], vec_rows[:, :], ident[0:N_VEC, 0:N_VEC]).then_inc(vec_ps, 1)
            project(QKV_CHUNKS, 0, wi_lo, hT_hi, hT_lo, proj_done, proj_kept)
            for t in range(TB):
                pe.wait_ge(proj_kept[t], QKV_CHUNKS)
            pe.wait_ge(vec_ready, 1)

            with pe.Fori(0, HEADS) as j:
                def conv(s, bank, k0, k1):
                    for k in range(k0, k1):
                        piece = 2 * s + k // HALF_KT
                        if k % HALF_KT == 0:
                            pe.wait_ge(wc_ready, PIECES * j + piece + 1)
                        ring = piece % PIECE_RING
                        last = split_products(ps[:, bank, :], wc_hi[:, ring, k % HALF_KT, :],
                                              wc_lo[:, ring, k % HALF_KT, :], hT_hi[:, k, :], hT_lo[:, k, :],
                                              k == 0, k == KT - 1)
                        if k == HALF_KT - 1:
                            last.then_inc(wc_half_used, 1)
                    if k1 == KT:
                        last.then_inc(conv_done[s], 1)

                def scores(qb):
                    pe.wait_ge(scores_read[qb % 2], 4 * j + 2 * (qb // 2))
                    for c in range(2):
                        last = mm(ps[:, 2 + 2 * (qb % 2) + c, 0:(qb + 1) * P],
                                  qkT[c * HD:(c + 1) * HD, 0, qb * P:(qb + 1) * P],
                                  qkT[c * HD:(c + 1) * HD, 1, 0:(qb + 1) * P], start=True, stop=True)
                    last.then_inc(scores_done, 1)

                def turn_a(qb):
                    pe.wait_ge(a_ready, TB * j + qb + 1)
                    pe.wait_ge(aT_ready, TB * j + qb)
                    for kb in range(qb + 1):
                        last = turn(ps[:, 6, kb * P:(kb + 1) * P], probs[:, qb % 2, 0, kb * P:(kb + 1) * P],
                                    ident[:, :])
                    last.then_inc(a_turned[qb % 2], 1)

                def apply_v(qb):
                    pe.wait_ge(aT_ready, TB * j + qb + 1)
                    for kb in range(qb + 1):
                        last = mm(ps[:, 7, qb * P:(qb + 1) * P], aT[:, qb % 2, kb * P:(kb + 1) * P],
                                  qkv[:, kb, bass.ds(j * P + 2 * ATTN, P)], start=(kb == 0), stop=(kb == qb))
                    last.then_inc(av_done[qb % 2], 1)

                pe.wait_ge(conv_gated, j)
                conv(0, 0, 0, KT)
                for i in range(2):
                    pe.wait_ge(qk_normed, 2 * j + i + 1)
                    if i == 0:
                        pe.wait_ge(o_out, j)
                    else:
                        pe.wait_ge(o_normed, j)
                    for t in range(TB):
                        last = turn(ps[:, 6 + i, t * P:(t + 1) * P], qk_n[:, i, t * P:(t + 1) * P], ident[:, :])
                    last.then_inc(qkT_ps, 1)
                pe.wait_ge(c_kept, j)
                conv(1, 1, 0, 4)
                pe.wait_ge(qkT_ready, 2 * j + 2)
                scores(0)
                scores(1)
                conv(1, 1, 4, 10)
                turn_a(0)
                scores(2)
                conv(1, 1, 10, KT)
                apply_v(0)
                turn_a(1)
                scores(3)
                pe.wait_ge(b_kept, j + 1)
                conv(2, 0, 0, 5)
                apply_v(1)
                turn_a(2)
                conv(2, 0, 5, 10)
                apply_v(2)
                turn_a(3)
                conv(2, 0, 10, 13)
                apply_v(3)
                conv(2, 0, 13, KT)
                pe.wait_ge(o_normed, j + 1)
                for t in range(TB):
                    last = turn(ps[:, 6, t * P:(t + 1) * P], o_n[:, t * P:(t + 1) * P], ident[:, :])
                last.then_inc(oT_ps, 1)
            pe.wait_ge(o_out, HEADS)
            project(OUT_CHUNKS, QKV_CHUNKS, wo_lo, mix_hi, mix_lo, out_done, out_added, MIX_ORDER)
            norm(1)
            pe.wait_ge(hT_ready, 8 * TB)

            def queries(h, c, quarter, high=wq_hi, low=wq_lo):
                if quarter == 0:
                    pe.wait_ge(wq_ready, 2 * h + c + 1)
                    pe.wait_ge(*((key_scores_ready, 2 * h) if c == 0 else (pqT_ready, 2 * h + 1)))
                for k in range(4 * quarter, 4 * quarter + 4):
                    last = split_products(ps_pq, high[:, k, :], low[:, k, :], h2T_hi[:, k, :], h2T_lo[:, k, :],
                                          k == 0, k == KT - 1)
                if quarter == 3:
                    last.then_inc(wq_used, 1)

            def turn_keys(h):
                pe.wait_ge(keys_in, 16 * h + 16)
                pe.wait_ge(key_scores_ready, 2 * h)
                for c in range(2):
                    last = turn(ps_keysT[:, c, :], keys[:, c, :], ident[:, :])
                last.then_inc(keys_used, 1)

            def score_keys(h, c):
                pe.wait_ge(pqT_ready, 2 * h + c + 1)
                pe.wait_ge(keysT_ready, h + 1)
                for t in range(TB):
                    last = mm(ps_key_scores[c][:, t, :], pqT[:, c, t * P:(t + 1) * P], keysT[:, c, :],
                              start=True, stop=True)
                last.then_inc(key_scores_ps, 1)

            with pe.Fori(0, 2) as h:
                for quarter in range(4):
                    queries(h, 0, quarter, wq0_hi, wq0_lo)
                turn_keys(h)
                for quarter in range(4):
                    queries(h, 1, quarter)
                score_keys(h, 0)
                score_keys(h, 1)

            def turned(buffer, use, half):
                if half == 0:
                    pe.wait_ge(u_tile_in[buffer], 16 * use)
                for k in range(8):
                    last = turn(ps_uT[half][:, k, :], u_tile[buffer][:, (8 * half + k) * P:(8 * half + k + 1) * P],
                                ident[:, :])
                last.then_inc(uT_half0_ps if half == 0 else uT_half1_ps[buffer], 1)

            def sweep(i, querying, last=False):
                for b in range(TOPK):
                    c = TOPK * i + b
                    more = not (last and b == TOPK - 1)
                    nxt = (b + 1) % 2
                    for half in range(2):
                        pe.wait_ge(uT_ready[half], c + 1)
                        if half == 0:
                            pe.wait_ge(swept_kept[b % 2], TOPK // 2 * i + b // 2)
                        for k in range(8):
                            summed = split_products(ps[:, 4 + b % 2, 0:SWEPT], uT_hi[half][:, k, :],
                                                    uT_lo[half][:, k, :], h2T_hi[:, 8 * half + k, P:SEQ],
                                                    h2T_lo[:, 8 * half + k, P:SEQ],
                                                    half == 0 and k == 0, half == 1 and k == 7)
                        if half == 1:
                            summed.then_inc(swept[b % 2], 1)
                        if more:
                            turned(nxt, TOPK // 2 * i + (b + 1) // 2 + 1, half)
                    if querying:
                        for c in range(2):
                            if 0 <= b - QUERIES[c] < 4:
                                queries(i + 2, c, b - QUERIES[c])
                            if b == KEY_SCORES[c]:
                                score_keys(i + 2, c)
                        if b == KEYS_TURNED:
                            turn_keys(i + 2)

            turned(0, 1, 0)
            turned(0, 1, 1)
            with pe.Fori(0, PEER_HEADS - 2) as i:
                sweep(i, querying=True)
            sweep(PEER_HEADS - 2, querying=False)
            sweep(PEER_HEADS - 1, querying=False, last=True)

            def head(h, last):
                for t in range(1, TB):
                    n = SWEPT_BLOCKS * h + t - 1
                    pe.wait_ge(diag_ready, n + 1)
                    pe.wait_ge(rows_added, n)
                    for s in range(TOPK):
                        if s % 4 == 3:
                            continue
                        pe.wait_ge(v_in[s % RING], 16 * (TOPK // RING * n + s // RING + 1))
                        for m in range(D // CHUNK):
                            added = mm(ps[:, m, :], diag[:, s // 4, s % 4, :],
                                       v_ring[s % RING][:, m * CHUNK:(m + 1) * CHUNK],
                                       start=(s == 0), stop=(s == TOPK - 2))
                        added.then_inc(v_used[s % RING], 1)

            with pe.Fori(0, PEER_HEADS - 1) as h:
                head(h, last=False)
            head(PEER_HEADS - 1, last=True)


_INS = ["x", "attn_norm_g", "w_in", "q_norm_g", "k_norm_g", "lambda_q1", "lambda_k1", "lambda_q2", "lambda_k2",
        "subln_g", "conv_w", "w_out", "ffn_norm_g", "peer_w_q", "peer_subkeys", "peer_u", "peer_v"]


def kernel(**inputs):
    import numpy as _np
    import concourse.bacc as _bacc
    from concourse.bass_utils import run_bass_kernel_spmd as _run

    nc = _bacc.Bacc("TRN2", target_bir_lowering=False, num_devices=1)
    arrays, args = {}, []
    for name in _INS:
        a = _np.ascontiguousarray(inputs[name])
        arrays[f"in_{name}"] = a
        args.append(nc.dram_tensor(f"in_{name}", a.shape, mybir.dt.from_np(a.dtype), kind="ExternalInput").ap())
    args.append(nc.dram_tensor("out", (1, SEQ, D), F32, kind="ExternalOutput").ap())
    decoder_layer(nc, *args)
    return _run(nc, [arrays], core_ids=[0]).results[0]["out"]
```
